# Optimizing a Trainium2 kernel written in Bass

```python
import math
import jax, jax.numpy as jnp
from jax import lax
import numpy as np

D_MODEL = 2048
BATCH = 1
SEQ = 256
DEPTH = 1

CHUNK = 64
Q_BLOCK = 128
MAX_OFFSET = 65536

MLA_HEADS = 8
Q_LORA = 512
KV_LORA = 256
NOPE_DIM = 128
ROPE_DIM = 64
V_DIM = 128
ROPE_THETA = 10000.0

FOX_HEADS = 8
FOX_HEAD_DIM = 128

D_FF = 5632
CONV_WIDTH = 3

N_BRANCHES = 2
EPS = 1e-6
NEG_INF = -1e30

SPLITS = (
    Q_LORA,
    KV_LORA,
    ROPE_DIM,
    FOX_HEADS * FOX_HEAD_DIM,
    FOX_HEADS * FOX_HEAD_DIM,
    FOX_HEADS * FOX_HEAD_DIM,
    FOX_HEADS,
    N_BRANCHES * D_MODEL,
)
D_IN = sum(SPLITS)

kernel_name = "hybrid_mla_fox_convffn_block"

def rmsnorm(x, g):
    xf = x.astype(jnp.float32)
    y = xf * lax.rsqrt(jnp.mean(xf * xf, axis=-1, keepdims=True) + EPS)
    return (y * g.astype(jnp.float32)).astype(x.dtype)

def rope(x, cos, sin):
    half = x.shape[-1] // 2
    x1, x2 = x[..., :half], x[..., half:]
    return jnp.concatenate([x1 * cos - x2 * sin, x2 * cos + x1 * sin], axis=-1)

def rope_tables(positions, dtype):
    inv_freq = 1.0 / (ROPE_THETA ** (jnp.arange(0, ROPE_DIM, 2, dtype=jnp.float32) / ROPE_DIM))
    ang = positions.astype(jnp.float32)[..., None] * inv_freq
    return jnp.cos(ang).astype(dtype), jnp.sin(ang).astype(dtype)

def block_attention(q, k, v, causal_unit, log_decay=None):
    S = q.shape[1]
    scale = q.shape[-1] ** -0.5
    pos = jnp.arange(S)
    outs = []
    for i in range(S // Q_BLOCK):
        start, end = i * Q_BLOCK, (i + 1) * Q_BLOCK
        s = jnp.einsum('bqhd,bkhd->bhqk', q[:, start:end], k[:, :end]).astype(jnp.float32) * scale
        if log_decay is not None:
            s = s + log_decay[:, :, start:end, None] - log_decay[:, :, None, :end]
        visible = (pos[None, :end] // causal_unit) <= (pos[start:end, None] // causal_unit)
        s = jnp.where(visible, s, NEG_INF)
        p = jax.nn.softmax(s, axis=-1)
        outs.append(jnp.einsum('bhqk,bkhd->bqhd', p.astype(v.dtype), v[:, :end]))
    return jnp.concatenate(outs, axis=1)

def setup_inputs(seed: int = 0) -> dict:
    key = jax.random.key(seed)
    ks = jax.random.split(key, 24)
    f32 = jnp.float32
    nrm = lambda k, shape, fan_in: jax.random.normal(k, shape, f32) * (fan_in ** -0.5)
    gain = lambda k, n: 1.0 + 0.05 * jax.random.normal(k, (n,), f32)
    offset = jax.random.randint(ks[1], (BATCH, 1), 0, MAX_OFFSET, dtype=jnp.int32)
    positions = offset + jnp.arange(SEQ, dtype=jnp.int32)[None, :]
    return {
        "x": jax.random.normal(ks[0], (BATCH, SEQ, D_MODEL), f32),
        "positions": positions,
        "pre_mix_norm": gain(ks[2], D_MODEL),
        "w_in": nrm(ks[3], (D_MODEL, D_IN), D_MODEL),
        "q_a_norm": gain(ks[4], Q_LORA),
        "w_uq": nrm(ks[5], (Q_LORA, MLA_HEADS * (NOPE_DIM + ROPE_DIM)), Q_LORA),
        "kv_a_norm": gain(ks[6], KV_LORA),
        "w_ukv": nrm(ks[7], (KV_LORA, MLA_HEADS * (NOPE_DIM + V_DIM)), KV_LORA),
        "b_forget": jax.random.uniform(ks[8], (FOX_HEADS,), f32, 1.0, 4.0),
        "b_gate": 0.02 * jax.random.normal(ks[9], (N_BRANCHES * D_MODEL,), f32),
        "w_branch_mla": nrm(ks[10], (MLA_HEADS * V_DIM, D_MODEL), MLA_HEADS * V_DIM),
        "w_branch_fox": nrm(ks[11], (FOX_HEADS * FOX_HEAD_DIM, D_MODEL), FOX_HEADS * FOX_HEAD_DIM),
        "w_out": nrm(ks[12], (D_MODEL, D_MODEL), D_MODEL),
        "post_mix_norm": gain(ks[13], D_MODEL),
        "pre_ffn_norm": gain(ks[14], D_MODEL),
        "w_up": nrm(ks[15], (D_MODEL, 2 * D_FF), D_MODEL),
        "conv_w": nrm(ks[16], (CONV_WIDTH, 2 * D_FF), CONV_WIDTH),
        "conv_b": 0.02 * jax.random.normal(ks[17], (2 * D_FF,), f32),
        "w_down": nrm(ks[18], (D_FF, D_MODEL), D_FF),
        "post_ffn_norm": gain(ks[19], D_MODEL),
    }

def reference(x, positions, pre_mix_norm, w_in, q_a_norm, w_uq, kv_a_norm, w_ukv,
              b_forget, b_gate, w_branch_mla, w_branch_fox, w_out, post_mix_norm,
              pre_ffn_norm, w_up, conv_w, conv_b, w_down, post_ffn_norm):
    B, S, _ = x.shape
    cos, sin = rope_tables(positions, x.dtype)
    for _layer in range(DEPTH):
        h = rmsnorm(x, pre_mix_norm)
        proj = h @ w_in
        cuts = np.cumsum(SPLITS)[:-1].tolist()
        q_lat, kv_lat, k_pe, fq, fk, fv, f_logit, g_logit = jnp.split(proj, cuts, axis=-1)

        q = (rmsnorm(q_lat, q_a_norm) @ w_uq).reshape(B, S, MLA_HEADS, NOPE_DIM + ROPE_DIM)
        q_nope, q_pe = q[..., :NOPE_DIM], q[..., NOPE_DIM:]
        q_pe = rope(q_pe, cos[:, :, None, :], sin[:, :, None, :])
        kv = (rmsnorm(kv_lat, kv_a_norm) @ w_ukv).reshape(B, S, MLA_HEADS, NOPE_DIM + V_DIM)
        k_nope, v_mla = kv[..., :NOPE_DIM], kv[..., NOPE_DIM:]
        k_pe = rope(k_pe, cos, sin)[:, :, None, :]
        q_mla = jnp.concatenate([q_nope, q_pe], axis=-1)
        k_mla = jnp.concatenate([k_nope, jnp.broadcast_to(k_pe, (B, S, MLA_HEADS, ROPE_DIM))], axis=-1)
        o_mla = block_attention(q_mla, k_mla, v_mla, CHUNK).reshape(B, S, MLA_HEADS * V_DIM)

        log_f = jax.nn.log_sigmoid(f_logit.astype(jnp.float32) + b_forget.astype(jnp.float32))
        c = jnp.transpose(jnp.cumsum(log_f, axis=1), (0, 2, 1))
        shp = (B, S, FOX_HEADS, FOX_HEAD_DIM)
        o_fox = block_attention(fq.reshape(shp), fk.reshape(shp), fv.reshape(shp), 1, c)
        o_fox = o_fox.reshape(B, S, FOX_HEADS * FOX_HEAD_DIM)

        gates = jax.nn.sigmoid((g_logit + b_gate).astype(jnp.float32)).astype(x.dtype)
        g_mla, g_fox = gates[..., :D_MODEL], gates[..., D_MODEL:]
        merged = g_mla * (o_mla @ w_branch_mla) + g_fox * (o_fox @ w_branch_fox)
        x = x + rmsnorm(merged @ w_out, post_mix_norm)

        h2 = rmsnorm(x, pre_ffn_norm)
        u = h2 @ w_up
        u_pad = jnp.pad(u, ((0, 0), (CONV_WIDTH - 1, 0), (0, 0)))
        u = sum(conv_w[j] * u_pad[:, j:j + S] for j in range(CONV_WIDTH)) + conv_b
        gate, val = u[..., :D_FF], u[..., D_FF:]
        ff = (jax.nn.gelu(gate, approximate=True) * val) @ w_down
        x = x + rmsnorm(ff, post_ffn_norm)
    return x


_drawn_inputs = setup_inputs


def setup_inputs(seed=0):
    import zlib

    import numpy as np

    out = dict(_drawn_inputs(seed))
    spreads = {}
    factors = {'q_a_norm': 4.224, 'kv_a_norm': 2.837, 'b_gate': 8.0, 'conv_b': 3.478}
    for name, (base, spread) in spreads.items():
        noise = np.random.default_rng([zlib.crc32(name.encode()), seed]).standard_normal(out[name].shape)
        drawn = base * np.exp(spread * noise) if base else spread * noise
        out[name] = __import__('jax').numpy.asarray(drawn.astype(out[name].dtype))
    for name, factor in factors.items():
        out[name] = (out[name] * factor).astype(out[name].dtype)
    return out
```

```python
import math
from contextlib import ExitStack

import concourse.bass as bass
import numpy as np
from concourse import mybir

F32 = mybir.dt.float32
F32R = mybir.dt.float32r
I32 = mybir.dt.int32
ACT = mybir.ActivationFunctionType
ALU = mybir.AluOpType
AX = mybir.AxisListType

P = 128
SEQ, D = 256, 2048
TT = SEQ // P
Q_LORA, KV_LORA, ROPE = 512, 256, 64
HEADS, HD = 8, 128
QH = HD + ROPE
D_FF = 5632
LAT_COLS = Q_LORA + KV_LORA + ROPE
FOX0 = LAT_COLS
FV0 = FOX0 + 2 * HEADS * HD
GATE0 = FV0 + HEADS * HD + HEADS
FV_COLS = HEADS * HD + HEADS
FV_BLOCKS = 3
FV_W = FV_COLS // FV_BLOCKS
EPS = 1e-6
SCALE_MLA = float(QH) ** -0.5
SCALE_FOX = float(HD) ** -0.5
HIDDEN_SCORE = -1e30
MLA_CHUNK = 64

KT = D // P
FF_TILES = D_FF // P
W = 512
KC = 4
QUADS = FF_TILES // 4
DOWN_CHUNKS = FF_TILES // KC
LAT_TILES = (Q_LORA + KV_LORA) // P

LAT_T = 0
FV_T = LAT_T + 8
UQ_T = FV_T + 4 * FV_BLOCKS
UKV_T = UQ_T + 3
FQK_T = UQ_T + 8
GATES_T = FQK_T + 16
BRANCH_T = GATES_T + 32
OUT_T = BRANCH_T + 16
UP_T = OUT_T + 16
DOWN_T = UP_T + 8 * QUADS
END_T = DOWN_T + 4 * 12
HALVES = [2] * END_T
for _t in range(UKV_T + 2, FQK_T):
    HALVES[_t] = 0
for _j in range(4):
    HALVES[DOWN_T + 12 * _j + 11] = 0
BEFORE = [0]
for _h in HALVES:
    BEFORE.append(BEFORE[-1] + _h)


def halves_by(turn, half=2):
    if turn < 0:
        return 0
    return BEFORE[turn] + min(half, HALVES[turn])


def loads_by(turn):
    return sum(1 for t in range(turn % 4, turn + 1, 4) if HALVES[t])


class Turn:

    def __init__(self, first, per=0, i=0, span=None):
        self.first, self.per, self.i, self.span = first, per, i, span

    def plus(self, n):
        return Turn(self.first + n, self.per, self.i, self.span)

    def value(self, f):
        if isinstance(self.i, int):
            return f(self.first + self.per * self.i)
        v = [f(self.first + self.per * k) for k in self.span]
        step = v[-1] - v[-2]
        return self.i * step + max(x - step * k for x, k in zip(v, self.span))

    def slot(self):
        return self.first % 4

    def half_slot(self, half):
        return (2 * self.first + half) % 4

    def loaded(self):
        return 16 * self.value(loads_by) if isinstance(self.i, int) else self.value(lambda t: 16 * loads_by(t))

    def upto(self, half):
        return self.value(lambda t: halves_by(t, half + 1))

    def slot_freed(self):
        return self.value(lambda t: halves_by(t - 4))

    def half_freed(self, half):
        return self.value(lambda t: halves_by(t - 2, half + 1))


class Own:

    def __init__(self, eng, sem):
        self.eng, self.sem, self.n, self.i, self.a, self.per = eng, sem, 0, None, 0, 0

    def enter(self, i, a, per):
        self.i, self.a, self.per, self.start = i, a, per, self.n

    def leave(self, count):
        assert self.n - self.start == self.per, (self.n - self.start, self.per)
        self.n = self.start + self.per * count
        self.i = None

    def done(self, ins):
        ins.then_inc(self.sem, 1)
        self.n += 1
        if self.i is None:
            self.eng.wait_ge(self.sem, self.n)
        else:
            self.eng.wait_ge(self.sem, self.i * self.per + (self.n - self.a * self.per))


def residual_block(nc, x, positions, pre_mix_norm, w_in, q_a_norm, w_uq, kv_a_norm, w_ukv, b_forget,
                   b_gate, w_branch_mla, w_branch_fox, w_out, post_mix_norm, pre_ffn_norm, w_up,
                   conv_w, conv_b, w_down, post_ffn_norm, inv_freq, out):
    ctx = ExitStack()
    with ctx:
        place = [16512]

        def at(name, shape, dt, offset):
            return nc.alloc_sbuf_tensor_at(name, shape, dt, offset=offset)

        def sem(name):
            return ctx.enter_context(nc.semaphore(name))

        KB = 1024
        base = 16512
        raw = at("raw", [P, 4, KC, W], F32, base)
        hi = at("hi", [P, 4, 2, W], F32R, base + 32 * KB)
        lo = at("lo", [P, 4, 2, W], F32R, base + 48 * KB)
        body = base + 64 * KB
        xs = at("xs", [P, TT, D], F32, body)
        lat_nat = at("lat_nat", [P, TT, LAT_COLS], F32, body)
        rope_tmp = at("rope_tmp", [P, 4, TT, HEADS, ROPE // 2], F32, body + 7 * KB)
        probs = at("probs", [P, 2, 384], F32, body)
        probsT = at("probsT", [P, 2, 384], F32, body + 3 * KB)
        q_now = at("q_now", [P, 2, SEQ], F32, body + 6 * KB)
        qpe_now = at("qpe_now", [P, SEQ], F32, body + 8 * KB)
        v_now = at("v_now", [P, 2, TT, HD], F32, body + 9 * KB)
        head_row = at("head_row", [HEADS, P], F32, body + 11 * KB)
        B = body + 16 * KB
        hT = at("hT", [P, KT, 2, SEQ], F32R, B)
        mergedT = at("mergedT", [P, KT, 2, SEQ], F32R, B)
        h2T = at("h2T", [P, KT, 2, SEQ], F32R, B)
        y_ffn = at("y_ffn", [P, TT, D], F32, B)
        ffn_gain = at("ffn_gain", [P, D], F32, B + 16 * KB)
        ffn_junk = at("ffn_junk", [P, 2 * W], F32, B + 24 * KB)
        C = B + 32 * KB
        fqkT = at("fqkT", [P, HEADS, 2, SEQ], F32, C)
        o_foxT = at("o_foxT", [P, HEADS, 2, SEQ], F32R, C)
        vf = at("vf", [P, TT, FV_COLS], F32, C + 16 * KB)
        m_mla = at("m_mla", [P, TT, W], F32, C + 16 * KB)
        m_fox = at("m_fox", [P, TT, W], F32, C + 20 * KB)
        E = C + 16 * KB + 8448
        qkT = at("qkT", [P, HEADS, 2, SEQ], F32, E)
        o_mlaT = at("o_mlaT", [P, HEADS, 2, SEQ], F32R, E)
        qpeT = at("qpeT", [P, HEADS // 2, SEQ], F32, E + 16 * KB)
        kpeT = at("kpeT", [P, SEQ], F32, E + 20 * KB)
        v_mla = at("v_mla", [P, TT, HEADS, HD], F32, E + 21 * KB)
        mix_gain = at("mix_gain", [P, D], F32, E + 21 * KB)
        G = E + 29 * KB
        q_nat = at("q_nat", [P, TT, HEADS, QH], F32, G)
        k_nat = at("k_nat", [P, TT, HEADS, HD], F32, G + 12 * KB)
        latT = at("latT", [P, LAT_TILES, 2, SEQ], F32R, G + 20 * KB)
        gates = at("gates", [P, TT, 2 * D], F32, G)
        y_mix = at("y_mix", [P, TT, D], F32, G)
        junk = at("junk", [P, D], F32, G + 16 * KB)
        tri_ones = at("tri_ones", [P, 2 * P], F32, G + 32 * KB)
        ffT = at("ffT", [P, FF_TILES, 2, SEQ], F32R, C)
        gate_act = at("gate_act", [P, FF_TILES, 2, SEQ], F32, C)
        J = body + 136 * KB
        assert G + 33 * KB <= J and C + 88 * KB <= J
        convp = at("convp", [P, 4, 2 * FF_TILES], F32, J)
        gcol = at("gcol", [P, 48], F32, J + 1408)
        small = at("small", [P, 64], F32, J + 1600)
        J2 = J + 1856
        ident = at("ident", [P, P], F32, J2)
        mask_fox = at("mask_fox", [P, P], F32, J2 + 512)
        mask_mla = at("mask_mla", [P, P], F32, J2 + 1024)
        bgate = at("bgate", [P, 2, W], F32, J2 + 1536)
        qpe_nat = at("qpe_nat", [P, TT, HEADS, ROPE], F32, J2 + 1536)
        sc_end = J2 + 1536 + 4096
        kpe_nat = at("kpe_nat", [P, TT, 2, ROPE], F32, body + 15 * KB)
        gain_rows = at("gain_rows", [38, P], F32, E)
        conv_rows = at("conv_rows", [88, 4, P], F32, E + 512)
        angle = at("angle", [P, 6, TT, ROPE // 2], F32, E + 3 * KB)
        inv_sb = at("inv_sb", [P, ROPE // 2], F32, E + 5 * KB)
        pos_i = at("pos_i", [P, TT], I32, E + 5 * KB + 128)
        fgt = at("fgt", [P, 4, TT, HEADS], F32, G + 34 * KB)
        negc = at("negc", [HEADS, SEQ], F32, body + 12 * KB)
        cossin = at("cossin", [P, 2, TT, ROPE // 2], F32, G + 33 * KB)
        bfor = at("bfor", [P, HEADS], F32, G + 34 * KB + 256)
        u_low = at("u_low", [P, 2, SEQ], F32, J2)
        u_pad = at("u_pad", [P, 2, SEQ + 2], F32, J2 + 2048)
        conv = at("conv", [P, 2, SEQ], F32, J2 + 4128)
        assert max(sc_end, J2 + 4128 + 2048) <= 229344 and G + 34 * KB + 320 <= J, (sc_end, G + 34 * KB + 320, J)

        EPS_C, ONE_C, SS_X, RS_X, SS_L, RS_L = 0, 1, 2, 4, 6, 10
        MX, NB, SUM, CQ, SS_O, SS_1, RS_1 = 14, 18, 22, 26, 42, 50, 54

        def col(c, n=1):
            return small[:, c:c + n]

        ps = ctx.enter_context(nc.psum_tensor("ps", [P, 8, 512], F32))

        chunk_loaded = [sem(f"chunk_loaded_{i}") for i in range(4)]
        hi_ready = sem("hi_ready")
        lo_ready = sem("lo_ready")
        halves_used = sem("halves_used")
        x_loaded = [sem(f"x_loaded_{t}") for t in range(TT)]
        gains_loaded, convs_loaded, rope_loaded = sem("gains_loaded"), sem("convs_loaded"), sem("rope_loaded")
        bfor_loaded = sem("bfor_loaded")
        bgate_loaded = [sem(f"bgate_loaded_{i}") for i in range(2)]
        mix_gain_loaded, x_again, ffn_gain_loaded = sem("mix_gain_loaded"), sem("x_again"), sem("ffn_gain_loaded")
        out_stored = sem("out_stored")
        consts = sem("consts")
        act_own, dve_own, pool_own = sem("act_own"), sem("dve_own"), sem("pool_own")
        squares = sem("squares")
        roots = sem("roots")
        normed = sem("normed")
        columns_done, columns_ready = sem("columns_done"), sem("columns_ready")
        angles_ready, sines_ready = sem("angles_ready"), sem("sines_ready")
        turned = sem("turned")
        parts_hi, parts_lo = sem("parts_hi"), sem("parts_lo")
        mix_act, mix_dve = sem("mix_act"), sem("mix_dve")
        q_roped, kpe_roped = sem("q_roped"), sem("kpe_roped")
        items_turned, items_act, items_dve = sem("items_turned"), sem("items_act"), sem("items_dve")
        forget_abs, forget_soft, forget_ready, decay_summed, decay_ready = (
            sem("forget_abs"), sem("forget_soft"), sem("forget_ready"), sem("decay_summed"), sem("decay_ready"))
        q_staged, v_staged = sem("q_staged"), sem("v_staged")
        scores_done, shifts_ready, probs_raw, probs_ready = (
            sem("scores_done"), sem("shifts_ready"), sem("probs_raw"), sem("probs_ready"))
        probs_turned, probsT_act, probsT_dve = sem("probs_turned"), sem("probsT_act"), sem("probsT_dve")
        heads_done, heads_hi, heads_lo = sem("heads_done"), sem("heads_hi"), sem("heads_lo")
        gate_sum, gates_ready = sem("gate_sum"), sem("gates_ready")
        merged_ready, merged_turned, merged_hi, merged_lo = (
            sem("merged_ready"), sem("merged_turned"), sem("merged_hi"), sem("merged_lo"))
        out_sq, out_evac = sem("out_sq"), sem("out_evac")
        res_ready, res_sq = sem("res_ready"), sem("res_sq")
        u_low_ready, ffn_evac, conv_ready = sem("u_low_ready"), sem("ffn_evac"), sem("conv_ready")
        branch_evac = sem("branch_evac")
        act_took_conv, ff_lo_ready = sem("act_took_conv"), sem("ff_lo_ready")
        down_sq = sem("down_sq")
        y_ready = sem("y_ready")

        block = ctx.enter_context(nc.Block())

        def k_view(w):
            return w.rearrange("(k p) c -> p k c", p=P)

        w_in_v, w_uq_v, w_ukv_v = k_view(w_in), k_view(w_uq), k_view(w_ukv)
        wbm_v, wbf_v, w_out_v = k_view(w_branch_mla), k_view(w_branch_fox), k_view(w_out)
        w_up_v, w_down_v = k_view(w_up), k_view(w_down)
        x_v = x[0].rearrange("(t p) d -> p t d", p=P)
        out_v = out[0].rearrange("(t p) d -> p t d", p=P)
        bgate_v = b_gate.rearrange("(a n) -> a n", a=1)

        def cols(w):
            return bass.ds(w, W) if not isinstance(w, int) else slice(w, w + W)

        def wide(turn):
            return raw[:, turn.slot(), :, :].rearrange("p (k b) c -> p k (b c)", k=2)

        def raw_half(turn, half, width, wide_chunk):
            if wide_chunk:
                return wide(turn)[:, :, W * half:W * half + W]
            return raw[:, turn.slot(), 2 * half:2 * half + 2, 0:width]

        def cos_sin(j):
            return cossin[:, j]

        def q_flat(t, j):
            return q_nat[:, t].rearrange("p h d -> p (h d)")[:, W * j:W * j + W]

        def heads_in_bank(bank):
            return ps[:, bank, :].rearrange("p (h d) -> p h d", h=2)

        def kv_bank(b):
            v = ps[:, b, :].rearrange("p (h d) -> p h d", h=2)
            return v[:, :, 0:HD], v[:, :, HD:2 * HD]

        def item_from(r):
            bank = ps[:, 4 + r % 4, :]
            return bank[:, 0:SEQ] if r == 4 else bank.rearrange("p (h q) -> p h q", h=2)

        def item_to(r):
            if r < 4:
                return qkT[:, 2 * r:2 * r + 2, 1, :]
            if r == 4:
                return kpeT[:]
            if r < 9:
                return qkT[:, 2 * (r - 5):2 * (r - 5) + 2, 0, :]
            return qpeT[:, 2 * (r - 9):2 * (r - 9) + 2, :]

        def fqk_to(j, b):
            h = 4 * (j % 2) + 2 * b
            return fqkT[:, h:h + 2, j // 2, :]

        def k_tiles(i, unit):
            k = i * 4 + 2 * unit
            return slice(k, k + 2) if isinstance(k, int) else bass.ds(k, 2)

        def one(h):
            return slice(h, h + 1) if isinstance(h, int) else bass.ds(h, 1)

        def span_of(c, n):
            return slice(c, c + n) if isinstance(c, int) else bass.ds(c, n)

        @block.sync
        def _(sp):
            def load(turn, src, n=KC, width=W):
                freed = turn.slot_freed()
                if not isinstance(freed, int) or freed > 0:
                    sp.wait_ge(lo_ready, freed)
                dst = raw[:, turn.slot(), 0:n, 0:width] if width <= W else wide(turn)
                sp.dma_start(dst, src).then_inc(chunk_loaded[turn.slot()], 16)

            def snap(c):
                return c if isinstance(c, int) else sp.snap(c)

            for t in range(TT):
                sp.dma_start(xs[:, t, :], x_v[:, t, :]).then_inc(x_loaded[t], 16)
            for j, (c0, width) in enumerate(((0, W), (W, LAT_COLS - W))):
                for c in range(4):
                    load(Turn(LAT_T + 4 * j + c), w_in_v[:, 4 * c:4 * c + 4, c0:c0 + width], KC, width)
                if j == 0:
                    with nc.allow_non_contiguous_dma(reason="256 positions"):
                        sp.dma_start(pos_i[:], positions.rearrange("b (t p) -> p (b t)", p=P))\
                          .then_inc(rope_loaded, 16)
                    sp.dma_start(inv_sb[:], inv_freq.to_broadcast([P, ROPE // 2])).then_inc(rope_loaded, 16)
                    sp.dma_start(bfor[:], b_forget.rearrange("(a n) -> a n", a=1).to_broadcast([P, HEADS]))\
                      .then_inc(bfor_loaded, 16)
                    sp.dma_start(conv_rows[:, 0:3, :], conv_w.rearrange("j (r c) -> r j c", c=P))\
                      .then_inc(convs_loaded, 16)
                    sp.dma_start(conv_rows[:, 3, :], conv_b.rearrange("(r c) -> r c", c=P)).then_inc(convs_loaded, 16)
            for j in range(FV_BLOCKS):
                for c in range(4):
                    c0 = FV0 + FV_W * j
                    load(Turn(FV_T + 4 * j + c), w_in_v[:, 4 * c:4 * c + 4, c0:c0 + FV_W], KC, FV_W)
            for j in range(3):
                load(Turn(UQ_T + j), w_uq_v[:, :, W * j:W * j + W])
            for j in range(2):
                load(Turn(UKV_T + j), w_ukv_v[:, :, 2 * W * j:2 * W * j + 2 * W], 2, 2 * W)
            for j in range(4):
                for c in range(4):
                    c0 = FOX0 + W * j
                    load(Turn(FQK_T + 4 * j + c), w_in_v[:, 4 * c:4 * c + 4, c0:c0 + W])

            def gate_loads(p, span):
                for s in range(2):
                    if not isinstance(p, int):
                        sp.wait_ge(gate_sum, p * 4 + (2 * s - 2))
                    else:
                        sp.wait_ge(items_turned, 11)
                    sp.dma_start(bgate[:, s, :], bgate_v[:, cols(p * (2 * W) + W * s)].to_broadcast([P, W]))\
                      .then_inc(bgate_loaded[s], 16)
                    for c in range(4):
                        load(Turn(GATES_T + 4 * s + c, 8, p, span),
                             w_in_v[:, 4 * c:4 * c + 4, cols(snap(p * (2 * W) + (GATE0 + W * s)))])

            gate_loads(0, None)
            with sp.Fori(1, 4) as p:
                gate_loads(p, range(1, 4))
            for c in range(4):
                for b, wv in enumerate((wbm_v, wbf_v)):
                    for k in range(2):
                        load(Turn(BRANCH_T + 4 * c + 2 * b + k), wv[:, 4 * k:4 * k + 4, W * c:W * c + W])
            for j in range(4):
                for c in range(4):
                    load(Turn(OUT_T + 4 * j + c), w_out_v[:, 4 * c:4 * c + 4, W * j:W * j + W])
                if j == 0:
                    sp.wait_ge(heads_lo, 2 * HEADS)
                    sp.wait_ge(heads_hi, 2 * HEADS)
                    sp.dma_start(mix_gain[:], post_mix_norm.rearrange("(a n) -> a n", a=1).to_broadcast([P, D]))\
                      .then_inc(mix_gain_loaded, 16)
                    sp.dma_start(xs[:], x_v).then_inc(x_again, 16)

            def up_loads(i, span):
                for s in range(2):
                    for c in range(4):
                        load(Turn(UP_T + 4 * s + c, 8, i, span),
                             w_up_v[:, 4 * c:4 * c + 4, cols(snap(i * W + D_FF * s))])

            up_loads(0, None)
            with sp.Fori(1, QUADS) as i:
                up_loads(i, range(1, QUADS))
            with sp.Fori(0, 2) as p:
                for s in range(2):
                    for c in range(DOWN_CHUNKS):
                        load(Turn(DOWN_T + 12 * s + c, 24, p, range(2)),
                             w_down_v[:, 4 * c:4 * c + 4, cols(snap(p * (2 * W) + W * s))])
            for t in range(TT):
                for b in range(2):
                    sp.wait_ge(y_ready, 2 * t + b + 1)
                    sp.dma_start(out_v[:, t, 1024 * b:1024 * b + 1024], y_ffn[:, t, 1024 * b:1024 * b + 1024])\
                      .then_inc(out_stored, 16)
            sp.wait_ge(out_stored, 64)

        @block.gpsimd
        def _(pool):
            own = Own(pool, pool_own)
            own.done(pool.memset(ident[:], 0.0))
            own.done(pool.memset(tri_ones[:], 1.0))
            own.done(pool.memset(mask_fox[:], 0.0))
            own.done(pool.memset(mask_mla[:], 0.0))
            own.done(pool.memset(col(ONE_C), 1.0))
            own.done(pool.memset(col(EPS_C), EPS))
            pool.memset(mask_mla[0:MLA_CHUNK, MLA_CHUNK:P], HIDDEN_SCORE / SCALE_MLA).then_inc(consts, 1)
            pool.affine_select(out=ident[:], in_=ident[:], compare_op=ALU.not_equal, fill=1.0, base=0,
                               pattern=[[-1, P]], channel_multiplier=1).then_inc(consts, 1)
            pool.affine_select(out=tri_ones[:, 0:P], in_=tri_ones[:, 0:P], compare_op=ALU.is_ge, fill=0.0,
                               base=0, pattern=[[1, P]], channel_multiplier=-1).then_inc(consts, 1)
            pool.affine_select(out=mask_fox[:], in_=mask_fox[:], compare_op=ALU.is_ge,
                               fill=HIDDEN_SCORE / SCALE_FOX, base=0, pattern=[[-1, P]],
                               channel_multiplier=1).then_inc(consts, 1)

            def stage(h, p, par):
                if not isinstance(h, int) or h > 0:
                    pool.wait_ge(scores_done, h)
                own.done(pool.tensor_copy(q_now[:, 0, :], qkT[:, h, 0, :]))
                own.done(pool.tensor_copy(q_now[:, 1, :], fqkT[:, h, 0, :]))
                half = slice(64 * par, 64 * par + 64)
                own.done(pool.tensor_copy(qpe_now[half, :], qpeT[half, one(p), :].rearrange("a b q -> a (b q)")))
                own.done(pool.tensor_copy(head_row[:], ident[0:HEADS, one(h)].to_broadcast([HEADS, P])))
                pool.sem_inc(q_staged, 1)
                if not isinstance(h, int) or h > 0:
                    pool.wait_ge(heads_done, h)
                own.done(pool.tensor_copy(v_now[:, 0, :, :], v_mla[:, :, h, :]))
                own.done(pool.tensor_copy(v_now[:, 1, :, :], vf[:, :, span_of(h * HD, HD)]))
                pool.sem_inc(v_staged, 1)

            pool.wait_ge(mix_act, 15)
            pool.wait_ge(mix_dve, 15)
            pool.wait_ge(items_act, 6)
            pool.wait_ge(items_dve, 5)
            pool.wait_ge(decay_ready, 2)
            for s in range(2):
                stage(s, 0, s)
            pool.wait_ge(mix_act, 16)
            pool.wait_ge(mix_dve, 16)
            with pool.Fori(1, 4) as p:
                own.enter(p, 1, 12)
                for s in range(2):
                    stage(p * 2 + s, p, s)
            own.leave(3)
            pool.wait_ge(turned, 4 * KT + 2 * LAT_TILES)
            pool.memset(u_pad[:, :, 0:2], 0.0).then_inc(consts, 1)
            pool.wait_ge(halves_used, halves_by(DOWN_T - 1))
            pool.dma_start(ffn_gain[:], post_ffn_norm.rearrange("(a n) -> a n", a=1).to_broadcast([P, D]))\
                .then_inc(ffn_gain_loaded, 16)
            pool.wait_ge(ffn_gain_loaded, 16)

        @block.scalar
        def _(act):
            own = Own(act, act_own)
            A = nc.scalar.activation

            def split(turn, half, width=W, wide_chunk=False):
                act.wait_ge(chunk_loaded[turn.slot()], turn.loaded())
                freed = turn.half_freed(half)
                if not isinstance(freed, int) or freed > 0:
                    act.wait_ge(halves_used, freed)
                A(hi[:, turn.half_slot(half), :, 0:width], raw_half(turn, half, width, wide_chunk), ACT.Copy).then_inc(hi_ready, 1)

            act.dma_start(gain_rows[0:KT, :], pre_mix_norm.rearrange("(r c) -> r c", c=P)).then_inc(gains_loaded, 16)
            act.dma_start(gain_rows[KT:2 * KT, :], pre_ffn_norm.rearrange("(r c) -> r c", c=P)).then_inc(gains_loaded, 16)
            act.dma_start(gain_rows[32:36, :], q_a_norm.rearrange("(r c) -> r c", c=P)).then_inc(gains_loaded, 16)
            act.dma_start(gain_rows[36:38, :], kv_a_norm.rearrange("(r c) -> r c", c=P)).then_inc(gains_loaded, 16)
            act.wait_ge(consts, 1)
            A(col(RS_X), col(ONE_C), ACT.Sqrt)
            for t in range(TT):
                act.wait_ge(x_loaded[t], 16)
                own.done(A(junk[:], xs[:, t, :], ACT.Square, accum_out=col(SS_X + t)))
                A(col(RS_X + t), col(SS_X + t), ACT.Sqrt, scale=1.0 / D, bias=col(EPS_C)).then_inc(roots, 1)

            def parts_high(dst, n, first_turn, gain0):
                act.wait_ge(turned, first_turn + (TT * 4 + 2 * n + 2 if n < 4 else 4 * (n + 1)))
                for v in range(2):
                    k = 2 * n + v
                    A(dst[:, k, 0, :], ps[:, 4 + n % 4, 256 * v:256 * v + 256], ACT.Copy,
                      scale=gcol[:, gain0 + k:gain0 + k + 1]).then_inc(parts_hi, 1)

            def evac_lat(j):
                act.wait_ge(halves_used, halves_by(LAT_T + 4 * j + 3))
                c0, width = (0, W) if j == 0 else (W, LAT_COLS - W)
                A(lat_nat[:, 0, c0:c0 + width], ps[:, 2 * j, 0:width], ACT.Copy).then_inc(mix_act, 1)

            def evac_t0(job, turn, dst, width):
                act.wait_ge(halves_used, halves_by(turn))
                A(dst, ps[:, 2 * (job % 2), 0:width], ACT.Copy).then_inc(mix_act, 1)

            def evac_kv(j):
                act.wait_ge(halves_used, halves_by(UKV_T + j // 2, j % 2 + 1))
                keys, values = kv_bank(2 * (j % 2))
                A(k_nat[:, 0, 2 * j:2 * j + 2, :], keys, ACT.Copy)
                A(v_mla[:, 0, 2 * j:2 * j + 2, :], values, ACT.Copy).then_inc(mix_act, 1)

            def fqk_evac(j):
                act.wait_ge(halves_used, halves_by(FQK_T + 4 * j + 3))
                A(fqk_to(j, 0), heads_in_bank(2 * (j % 2)), ACT.Copy).then_inc(mix_act, 1)

            act.wait_ge(columns_ready, 1)
            for j, width in enumerate((W, LAT_COLS - W)):
                for n in range(8):
                    split(Turn(LAT_T + 4 * j + n // 2), n % 2, width)
                    if j == 0:
                        parts_high(hT, n, 0, 0)
                    if j == 1 and n == 3:
                        evac_lat(0)
                    if j == 1 and n == 5:
                        act.wait_ge(angles_ready, 2)
                        A(cos_sin(0), angle[:, 1], ACT.Sin).then_inc(sines_ready, 1)
                        A(cos_sin(1), angle[:, 2], ACT.Sin).then_inc(sines_ready, 1)
            for j in range(FV_BLOCKS):
                for n in range(8):
                    split(Turn(FV_T + 4 * j + n // 2), n % 2, FV_W)
                    if n == 3 and j == 0:
                        evac_lat(1)
                    elif n == 3:
                        evac_t0(1 + j, FV_T + 4 * j - 1, vf[:, 0, FV_W * (j - 1):FV_W * j], FV_W)
                    if j == 0 and n == 5:
                        act.wait_ge(mix_act, 2)
                        act.wait_ge(mix_dve, 2)
                        for t in range(TT):
                            A(junk[:, 0:Q_LORA], lat_nat[:, t, 0:Q_LORA], ACT.Square, accum_out=col(SS_L + t))
                            own.done(A(junk[:, 512:768], lat_nat[:, t, Q_LORA:Q_LORA + KV_LORA], ACT.Square,
                                       accum_out=col(SS_L + 2 + t)))
                        A(col(RS_L, 2), col(SS_L, 2), ACT.Sqrt, scale=1.0 / Q_LORA, bias=col(EPS_C))
                        A(col(RS_L + 2, 2), col(SS_L + 2, 2), ACT.Sqrt, scale=1.0 / KV_LORA,
                          bias=col(EPS_C)).then_inc(roots, 1)
                    if j == 1 and n == 5:
                        for k in range(LAT_TILES):
                            act.wait_ge(turned, 2 * KT + 2 * (k - k % 2) + 4)
                            A(latT[:, k, 0, :], ps[:, 4 + k // 2, 256 * (k % 2):256 * (k % 2) + 256], ACT.Copy,
                              scale=gcol[:, 32 + k:33 + k]).then_inc(parts_hi, 1)
            for j in range(3):
                for n in range(2):
                    split(Turn(UQ_T + j), n)
                if j == 1:
                    evac_t0(4, FV_T + 11, vf[:, 0, FV_W * 2:FV_W * 3], FV_W)
                if j == 2:
                    evac_t0(5, UQ_T, q_flat(0, 0), W)
            for j in range(4):
                split(Turn(UKV_T + j // 2), j % 2, W, True)
                if j > 0:
                    evac_t0(5 + j, UQ_T + j, q_flat(0, j), W) if j < 3 else evac_kv(0)
            evac_kv(1)
            for j in range(4):
                for n in range(8):
                    split(Turn(FQK_T + 4 * j + n // 2), n % 2)
                    if j == 0 and n < 2:
                        evac_kv(2 + n)
                    if j == 1 and n == 2:
                        act.wait_ge(forget_abs, 1)
                        own.done(A(fgt[:, 2], fgt[:, 1], ACT.Exp, scale=-1.0))
                        A(fgt[:, 2], fgt[:, 2], ACT.Ln, bias=col(ONE_C)).then_inc(forget_soft, 1)
                    if j > 0 and n == 3:
                        fqk_evac(j - 1)
                    r = (8 * j + n - 5) // 2
                    if (8 * j + n - 5) % 2 == 0 and 0 <= r < 12 and r % 2 == 0:
                        act.wait_ge(items_turned, r + 1)
                        A(item_to(r), item_from(r), ACT.Copy).then_inc(items_act, 1)

            def gate_job(p, s, span, prev):
                h = p * 2 + s
                for n in range(8):
                    split(Turn(GATES_T + 4 * s + n // 2, 8, p, span), n % 2)
                    if n == 3:
                        if prev == "fqk":
                            fqk_evac(3)
                        else:
                            for t in range(TT):
                                act.wait_ge(gate_sum, h * 2 + (t - 1))
                                g = gates[:, t, cols(h * W - W)]
                                A(g, g, ACT.Tanh, scale=0.5).then_inc(gates_ready, 1)
                    if n == 4:
                        act.wait_ge(shifts_ready, h + 1)
                        if not isinstance(h, int) or h > 0:
                            act.wait_ge(probs_turned, h)
                        for b, sc in enumerate((SCALE_MLA, SCALE_FOX)):
                            for q in range(TT):
                                w = slice(128 * q, 128 + 256 * q)
                                last = A(probs[:, b, w], ps[:, 4 + b, w], ACT.Exp, scale=sc,
                                         bias=col(NB + 2 * b + q), accum_out=col(SUM + 2 * b + q))
                            last.then_inc(probs_raw, 1)
                    if n == 7:
                        act.wait_ge(probs_turned, h + 1)
                        A(probsT[:, 0, :], ps[:, 6, 0:384], ACT.Copy).then_inc(probsT_act, 1)
                act.wait_ge(heads_done, h + 1)
                A(o_mlaT[:, h, 0, :], ps[:, 4, 0:SEQ], ACT.Copy).then_inc(heads_hi, 1)
                A(o_foxT[:, h, 0, :], ps[:, 5, 0:SEQ], ACT.Copy).then_inc(heads_hi, 1)

            gate_job(0, 0, None, "fqk")
            gate_job(0, 1, None, "gate")
            with act.Fori(1, 4) as p:
                for s in range(2):
                    gate_job(p, s, range(1, 4), "gate")

            def merged_evac(c):
                for u in range(2):
                    act.wait_ge(merged_turned, 2 * c + u + 1)
                    A(mergedT[:, 4 * c + 2 * u:4 * c + 2 * u + 2, 0, :],
                      ps[:, 4 + (2 * c + u) % 4, :].rearrange("p (k q) -> p k q", k=2),
                      ACT.Copy, scale=0.5).then_inc(merged_hi, 1)

            for c in range(4):
                for n in range(8):
                    split(Turn(BRANCH_T + 4 * c + n // 2), n % 2)
                    if c == 0 and n == 3:
                        for t in range(TT):
                            act.wait_ge(gate_sum, 2 * 7 + t + 1)
                            g = gates[:, t, 7 * W:8 * W]
                            A(g, g, ACT.Tanh, scale=0.5).then_inc(gates_ready, 1)
                    if c > 0 and n == 6:
                        merged_evac(c - 1)

            def out_squares(j):
                act.wait_ge(halves_used, halves_by(OUT_T + 4 * j + 3))
                for t in (1, 0):
                    if t == 0:
                        act.wait_ge(out_evac, 2 * j + 1)
                    A(junk[:, W * t:W * t + W], ps[:, 2 * (j % 2) + t, :], ACT.Square,
                      accum_out=col(SS_O + 4 * t + j)).then_inc(out_sq, 1)

            for j in range(4):
                for n in range(8):
                    split(Turn(OUT_T + 4 * j + n // 2), n % 2)
                    if j == 0 and n == 5:
                        merged_evac(3)
                    if j > 0 and n == 3:
                        out_squares(j - 1)
                    if j == 3 and n == 5:
                        A(col(RS_L), col(ONE_C), ACT.Sqrt)
            for n in range(3):
                split(Turn(UP_T + n // 2), n % 2)
            out_squares(3)
            for t in range(TT):
                act.wait_ge(squares, t + 1)
                A(col(RS_X + t), col(SS_X + t), ACT.Sqrt, scale=1.0 / D, bias=col(EPS_C)).then_inc(roots, 1)
            split(Turn(UP_T + 1), 1)
            for t in range(TT):
                for b in range(2):
                    act.wait_ge(res_ready, 2 * t + b + 1)
                    A(junk[:, 1024 * b:1024 * b + 1024], xs[:, t, 1024 * b:1024 * b + 1024], ACT.Square,
                      accum_out=col(SS_1 + 2 * t + b)).then_inc(res_sq, 1)
                act.wait_ge(squares, TT + t + 1)
                A(col(RS_1 + t), col(RS_1 + t), ACT.Sqrt, scale=1.0 / D, bias=col(EPS_C)).then_inc(roots, 1)

            def low_parts(job, unit, turn):
                act.wait_ge(halves_used, turn.upto(1))
                n = job * 2 + unit
                if not isinstance(n, int) or n > 0:
                    act.wait_ge(ffn_evac, n)
                b = 4 * (job_set[0]) + 2 * unit
                A(u_low[:], ps[:, b:b + 2, 256:512], ACT.Copy).then_inc(u_low_ready, 1)

            job_set = [0]

            def gelu(i, unit):
                act.wait_ge(conv_ready, i * 4 + (unit + 1))
                A(gate_act[:, k_tiles(i, unit), 1, :], conv[:], ACT.Gelu_apprx_tanh).then_inc(act_took_conv, 1)

            def ff_hi(i, unit):
                act.wait_ge(conv_ready, i * 4 + (unit + 3))
                A(ffT[:, k_tiles(i, unit), 0, :], conv[:], ACT.Copy).then_inc(act_took_conv, 1)

            def up_job(i, s, span, prev):
                for n in range(8):
                    if isinstance(i, int) and s == 0:
                        if n >= 4:
                            split(Turn(UP_T + n // 2), n % 2)
                        parts_high(h2T, n, 2 * KT + 2 * LAT_TILES, KT)
                    else:
                        split(Turn(UP_T + 4 * s + n // 2, 8, i, span), n % 2)
                    if prev:
                        up_evac_act(i, s, span, n)

            def up_evac_act(i, s, span, n):
                if s == 1:
                    job_set[0] = 0
                    done, job, step, who = Turn(UP_T + 3, 8, i, span), i * 2, gelu, i
                else:
                    job_set[0] = 1
                    done, job, step, who = Turn(UP_T - 1, 8, i, span), i * 2 - 1, ff_hi, i - 1
                if n in (3, 5):
                    low_parts(job, (n - 3) // 2, done)
                if n in (4, 6):
                    step(who, (n - 4) // 2)

            up_job(0, 0, None, False)
            up_job(0, 1, None, True)
            with act.Fori(1, QUADS) as i:
                for s in range(2):
                    up_job(i, s, range(1, QUADS), True)

            def down_squares(j):
                act.wait_ge(halves_used, halves_by(DOWN_T + 12 * j + 11))
                for t in (1, 0):
                    if t == 0:
                        act.wait_ge(ffn_evac, 4 * QUADS + 2 * j + 1)
                    A(ffn_junk[:, W * t:W * t + W], ps[:, 2 * (j % 2) + t, :], ACT.Square,
                      accum_out=col(SS_O + 4 * t + j)).then_inc(down_sq, 1)

            for j in range(4):
                for n in range(2 * DOWN_CHUNKS):
                    split(Turn(DOWN_T + 12 * j + n // 2), n % 2)
                    if j == 0:
                        up_evac_act(QUADS, 0, None, n)
                    elif n == 3:
                        down_squares(j - 1)
                    if j == 3 and n == 8:
                        A(col(RS_L), col(ONE_C), ACT.Sqrt)
            down_squares(3)
            for t in range(TT):
                act.wait_ge(squares, 2 * TT + t + 1)
                A(col(RS_X + t), col(SS_X + t), ACT.Sqrt, scale=1.0 / D, bias=col(EPS_C)).then_inc(roots, 1)

        @block.vector
        def _(dve):
            own = Own(dve, dve_own)
            V = nc.vector
            STT = nc.vector.scalar_tensor_tensor

            def split(turn, half, width=W, wide_chunk=False):
                dve.wait_ge(hi_ready, turn.upto(half))
                V.tensor_tensor(lo[:, turn.half_slot(half), :, 0:width],
                                raw_half(turn, half, width, wide_chunk),
                                hi[:, turn.half_slot(half), :, 0:width].bitcast(F32), ALU.subtract).then_inc(lo_ready, 1)

            dve.wait_ge(columns_done, 1)
            V.tensor_copy(gcol[:, 0:38], ps[:, 0, 0:38]).then_inc(columns_ready, 1)
            for t in range(TT):
                dve.wait_ge(roots, t + 1)
                own.done(V.reciprocal(col(RS_X + t), col(RS_X + t)))
                V.tensor_scalar(xs[:, t, :], xs[:, t, :], col(RS_X + t), None, ALU.mult).then_inc(normed, 1)

            def low_of(dst, bank, half, gain):
                STT(out=dst[:, 1, :], in0=ps[:, bank, 256 * half:256 * half + 256], scalar=gain,
                    in1=dst[:, 0, :].bitcast(F32), op0=ALU.mult, op1=ALU.subtract).then_inc(parts_lo, 1)

            def parts_low(dst, n, before, gain0):
                dve.wait_ge(parts_hi, before + 2 * n + 2)
                for v in range(2):
                    k = 2 * n + v
                    low_of(dst[:, k], 4 + n % 4, v, gcol[:, gain0 + k:gain0 + k + 1])

            def rope_angles():
                dve.wait_ge(rope_loaded, 32)
                own.done(V.tensor_copy(col(RS_X, 2), pos_i[:]))
                for t in range(TT):
                    own.done(V.tensor_scalar(angle[:, 0, t, :], inv_sb[:], col(RS_X + t), None, ALU.mult))
                parts = (6.28125, 507 / 2.0 ** 18, 2 * math.pi - 6.28125 - 507 / 2.0 ** 18)
                magic = 1.5 * 2.0 ** 23
                for j, quarter in ((1, 0.0), (2, 0.25)):
                    turns, r = angle[:, 3], angle[:, j]
                    own.done(V.tensor_scalar(turns, angle[:, 0], 1 / (2 * math.pi), quarter, ALU.mult, ALU.add))
                    own.done(V.tensor_scalar(turns, turns, magic, None, ALU.add))
                    own.done(V.tensor_scalar(turns, turns, magic, None, ALU.subtract))
                    own.done(STT(out=r, in0=turns, scalar=-parts[0], in1=angle[:, 0], op0=ALU.mult, op1=ALU.add))
                    own.done(STT(out=r, in0=turns, scalar=-parts[1], in1=r, op0=ALU.mult, op1=ALU.add))
                    own.done(STT(out=r, in0=turns, scalar=-parts[2], in1=r, op0=ALU.mult, op1=ALU.add))
                    if quarter:
                        own.done(V.tensor_scalar(r, r, math.pi / 2, None, ALU.add))
                    V.tensor_scalar(r, r, 3.1415925, -3.1415925, ALU.min, ALU.max).then_inc(angles_ready, 1)

            def evac_t1(job, turn, dst, width):
                dve.wait_ge(halves_used, halves_by(turn))
                V.tensor_copy(dst, ps[:, 2 * (job % 2) + 1, 0:width]).then_inc(mix_dve, 1)

            def rope(dst, src, cos, sin, tmp):
                (d1, d2), (s1, s2) = dst, src
                V.tensor_tensor(tmp[0], s1, cos, ALU.mult)
                V.tensor_tensor(tmp[1], s2, sin, ALU.mult)
                V.tensor_tensor(tmp[2], s2, cos, ALU.mult)
                own.done(V.tensor_tensor(tmp[3], s1, sin, ALU.mult))
                V.tensor_tensor(d1, tmp[0], tmp[1], ALU.subtract)
                return V.tensor_tensor(d2, tmp[2], tmp[3], ALU.add)

            for j, width in enumerate((W, LAT_COLS - W)):
                for n in range(8):
                    split(Turn(LAT_T + 4 * j + n // 2), n % 2, width)
                    if j == 0:
                        parts_low(hT, n, 0, 0)
                    if j == 1 and n == 1:
                        rope_angles()
                    if j == 1 and n == 3:
                        evac_t1(0, LAT_T + 3, lat_nat[:, 1, 0:W], W)
                    if j == 1 and n == 6:
                        dve.wait_ge(columns_done, 2)
                        V.tensor_copy(convp[:].rearrange("p j f -> p (j f)"), ps[:, 4, 0:4 * 88])\
                         .then_inc(columns_ready, 1)
            H2 = ROPE // 2
            for j in range(FV_BLOCKS):
                for n in range(8):
                    split(Turn(FV_T + 4 * j + n // 2), n % 2, FV_W)
                    if n == 3 and j == 0:
                        evac_t1(1, LAT_T + 7, lat_nat[:, 1, W:LAT_COLS], LAT_COLS - W)
                    elif n == 3:
                        evac_t1(1 + j, FV_T + 4 * j - 1, vf[:, 1, FV_W * (j - 1):FV_W * j], FV_W)
                    if j == 0 and n == 6:
                        dve.wait_ge(roots, 3)
                        own.done(V.reciprocal(col(RS_L, 4), col(RS_L, 4)))
                        for t in range(TT):
                            q, kv = lat_nat[:, t, 0:Q_LORA], lat_nat[:, t, Q_LORA:Q_LORA + KV_LORA]
                            V.tensor_scalar(q, q, col(RS_L + t), None, ALU.mult)
                            V.tensor_scalar(kv, kv, col(RS_L + 2 + t), None, ALU.mult).then_inc(normed, 1)
                    if j == 0 and n == 7:
                        dve.wait_ge(sines_ready, 2)
                        for t in range(TT):
                            k1 = lat_nat[:, t, 768:768 + H2]
                            k2 = lat_nat[:, t, 768 + H2:768 + ROPE]
                            tmp = [rope_tmp[:, i, t, 0, :] for i in range(4)]
                            own.done(rope((kpe_nat[:, t, 0, 0:H2], kpe_nat[:, t, 0, H2:ROPE]), (k1, k2),
                                          cossin[:, 1, t, :], cossin[:, 0, t, :], tmp))
                            V.tensor_copy(kpe_nat[:, t, 1, :], kpe_nat[:, t, 0, :]).then_inc(kpe_roped, 1)
                    if j == 1 and n == 5:
                        for k in range(LAT_TILES):
                            dve.wait_ge(parts_hi, KT + k - k % 2 + 2)
                            low_of(latT[:, k], 4 + k // 2, k % 2, gcol[:, 32 + k:33 + k])
            for j in range(3):
                for n in range(2):
                    split(Turn(UQ_T + j), n)
                if j == 1:
                    evac_t1(4, FV_T + 11, vf[:, 1, FV_W * 2:FV_W * 3], FV_W)
                if j == 2:
                    evac_t1(5, UQ_T, q_flat(1, 0), W)

            def evac_kv(j):
                dve.wait_ge(halves_used, halves_by(UKV_T + j // 2, j % 2 + 1))
                keys, values = kv_bank(2 * (j % 2) + 1)
                V.tensor_copy(k_nat[:, 1, 2 * j:2 * j + 2, :], keys)
                V.tensor_copy(v_mla[:, 1, 2 * j:2 * j + 2, :], values).then_inc(mix_dve, 1)

            def fqk_evac(j):
                dve.wait_ge(halves_used, halves_by(FQK_T + 4 * j + 3))
                V.tensor_copy(fqk_to(j, 1), heads_in_bank(2 * (j % 2) + 1)).then_inc(mix_dve, 1)

            for j in range(4):
                split(Turn(UKV_T + j // 2), j % 2, W, True)
                if j > 0:
                    evac_t1(5 + j, UQ_T + j, q_flat(1, j), W) if j < 3 else evac_kv(0)
            evac_kv(1)

            def rope_queries(t):
                s1, s2 = q_nat[:, t, :, HD:HD + H2], q_nat[:, t, :, HD + H2:QH]
                cos = cossin[:, 1, t, :].unsqueeze(1).to_broadcast([P, HEADS, H2])
                sin = cossin[:, 0, t, :].unsqueeze(1).to_broadcast([P, HEADS, H2])
                tmp = [rope_tmp[:, i, t] for i in range(4)]
                rope((qpe_nat[:, t, :, 0:H2], qpe_nat[:, t, :, H2:ROPE]), (s1, s2), cos, sin, tmp)\
                    .then_inc(q_roped, 1)

            for j in range(4):
                for n in range(8):
                    split(Turn(FQK_T + 4 * j + n // 2), n % 2)
                    if j == 0 and n < 2:
                        evac_kv(2 + n)
                    if j == 1 and n == 1:
                        dve.wait_ge(mix_act, 5)
                        dve.wait_ge(mix_dve, 5)
                        dve.wait_ge(bfor_loaded, 16)
                        own.done(V.tensor_tensor(fgt[:, 0], vf[:, :, HEADS * HD:FV_COLS],
                                                 bfor[:].unsqueeze(1).to_broadcast([P, TT, HEADS]), ALU.add))
                        STT(out=fgt[:, 1], in0=fgt[:, 0], scalar=-1.0, in1=fgt[:, 0], op0=ALU.mult,
                            op1=ALU.max).then_inc(forget_abs, 1)
                    if j == 0 and n in (4, 6):
                        if n == 4:
                            dve.wait_ge(sines_ready, 2)
                            dve.wait_ge(mix_act, 8)
                            dve.wait_ge(mix_dve, 8)
                        rope_queries(n // 2 - 2)
                    if j == 1 and n == 4:
                        dve.wait_ge(forget_soft, 1)
                        STT(out=fgt[:, 3], in0=fgt[:, 0], scalar=0.0, in1=fgt[:, 2], op0=ALU.min,
                            op1=ALU.subtract).then_inc(forget_ready, 1)
                    if j > 0 and n == 3:
                        fqk_evac(j - 1)
                    r = (8 * j + n - 5) // 2
                    if (8 * j + n - 5) % 2 == 0 and 0 <= r < 12 and r % 2 == 1:
                        dve.wait_ge(items_turned, r + 1)
                        if r < 11:
                            V.tensor_copy(item_to(r), item_from(r)).then_inc(items_dve, 1)
                        else:
                            V.tensor_scalar(negc[:], ps[0:HEADS, 7, 0:SEQ], -1.0 / SCALE_FOX, None, ALU.mult)\
                             .then_inc(decay_ready, 1)
                            V.tensor_copy(small[:, CQ:CQ + 16].rearrange("p (h t) -> p t h", t=TT),
                                          ps[:, 7, SEQ:SEQ + 16].rearrange("p (t h) -> p t h", t=TT))\
                             .then_inc(decay_ready, 1)

            def gate_job(p, s, span, prev):
                h = p * 2 + s
                for n in range(8):
                    split(Turn(GATES_T + 4 * s + n // 2, 8, p, span), n % 2)
                    if n == 3:
                        if prev == "fqk":
                            fqk_evac(3)
                        else:
                            gate_evac(h - 1, 1 - s, p - 1 if s == 0 else p,
                                      Turn(GATES_T + 4 * s - 1, 8, p, span).upto(1))
                    if n == 4:
                        dve.wait_ge(scores_done, h + 1)
                        for q in range(TT):
                            last = V.reduce_max(small[:, MX + q:MX + q + 3:2], ps[:, 4:6, 128 * q:128 + 256 * q], AX.X)
                        own.done(last)
                        cq = small[:, span_of(h * 2 + CQ, 2)]
                        V.tensor_scalar(col(NB, 2), col(MX, 2), -SCALE_MLA, None, ALU.mult)
                        own.done(STT(out=col(MX + 2, 2), in0=col(MX + 2, 2), scalar=SCALE_FOX, in1=cq,
                                     op0=ALU.mult, op1=ALU.add))
                        V.tensor_tensor(col(NB + 2, 2), cq, col(MX + 2, 2), ALU.subtract).then_inc(shifts_ready, 1)
                    if n == 5:
                        dve.wait_ge(probs_raw, h * 2 + 2)
                        own.done(V.reciprocal(col(SUM, 4), col(SUM, 4)))
                        for b in range(2):
                            for q in range(TT):
                                w = probs[:, b, 128 * q:128 + 256 * q]
                                last = V.tensor_scalar(w, w, col(SUM + 2 * b + q), None, ALU.mult)
                        last.then_inc(probs_ready, 1)
                    if n == 7:
                        dve.wait_ge(probs_turned, h + 1)
                        V.tensor_copy(probsT[:, 1, :], ps[:, 7, 0:384]).then_inc(probsT_dve, 1)
                for b, o in enumerate((o_mlaT, o_foxT)):
                    dve.wait_ge(heads_hi, h * 2 + (b + 1))
                    V.tensor_tensor(o[:, one(h), 1, :].rearrange("p a q -> p (a q)"), ps[:, 4 + b, 0:SEQ],
                                    o[:, one(h), 0, :].rearrange("p a q -> p (a q)").bitcast(F32),
                                    ALU.subtract).then_inc(heads_lo, 1)

            def gate_evac(g, par, p, used):
                dve.wait_ge(halves_used, used)
                dve.wait_ge(bgate_loaded[par], p * 16 + 16)
                for t in range(TT):
                    V.tensor_tensor(gates[:, t, cols(g * W)], ps[:, 2 * par + t, :], bgate[:, par, :],
                                    ALU.add).then_inc(gate_sum, 1)

            gate_job(0, 0, None, "fqk")
            gate_job(0, 1, None, "gate")
            with dve.Fori(1, 4) as p:
                own.enter(p, 1, 6)
                for s in range(2):
                    gate_job(p, s, range(1, 4), "gate")
            own.leave(3)

            def branch_evac_job(c, b):
                dve.wait_ge(halves_used, halves_by(BRANCH_T + 4 * c + 2 * b + 1))
                dve.wait_ge(gates_ready, 2 * (4 * b + c) + 2)
                m = (m_mla, m_fox)[b]
                if b == 1 and c > 0:
                    dve.wait_ge(merged_turned, 2 * c)
                for t in range(TT):
                    ins = STT(out=m[:, t, :], in0=gates[:, t, D * b + W * c:D * b + W * c + W], scalar=1.0,
                              in1=ps[:, 2 * b + t, :], op0=ALU.add, op1=ALU.mult)
                    ins.then_inc(branch_evac, 1)
                if b == 1:
                    dve.wait_ge(branch_evac, 4 * c + 4)
                    V.tensor_tensor(m_fox[:], m_fox[:], m_mla[:], ALU.add).then_inc(merged_ready, 1)

            def merged_low(c):
                for u in range(2):
                    dve.wait_ge(merged_hi, 2 * c + u + 1)
                    k = 4 * c + 2 * u
                    STT(out=mergedT[:, k:k + 2, 1, :],
                        in0=ps[:, 4 + (2 * c + u) % 4, :].rearrange("p (k q) -> p k q", k=2), scalar=0.5,
                        in1=mergedT[:, k:k + 2, 0, :].bitcast(F32), op0=ALU.mult,
                        op1=ALU.subtract).then_inc(merged_lo, 1)

            for c in range(4):
                for n in range(8):
                    split(Turn(BRANCH_T + 4 * c + n // 2), n % 2)
                    if n == 3:
                        if c == 0:
                            gate_evac(7, 1, 3, halves_by(BRANCH_T - 1))
                        else:
                            branch_evac_job(c - 1, 1)
                    if n == 6 and c > 0:
                        merged_low(c - 1)
                    if n == 7:
                        branch_evac_job(c, 0)

            def out_evac_job(j):
                dve.wait_ge(halves_used, halves_by(OUT_T + 4 * j + 3))
                for t in range(TT):
                    if t == 1:
                        dve.wait_ge(out_sq, 2 * j + 1)
                    V.tensor_tensor(y_mix[:, t, W * j:W * j + W], ps[:, 2 * (j % 2) + t, :],
                                    mix_gain[:, W * j:W * j + W], ALU.mult).then_inc(out_evac, 1)

            for j in range(4):
                for n in range(8):
                    split(Turn(OUT_T + 4 * j + n // 2), n % 2)
                    if j == 0 and n == 3:
                        branch_evac_job(3, 1)
                    if j == 0 and n == 5:
                        merged_low(3)
                    if j > 0 and n == 3:
                        if j == 1:
                            dve.wait_ge(mix_gain_loaded, 16)
                        out_evac_job(j - 1)
            for n in range(3):
                split(Turn(UP_T + n // 2), n % 2)

            def total_squares(count, sq):
                dve.wait_ge(sq, count)
                for t in range(TT):
                    V.reduce_sum(col(SS_X + t), col(SS_O + 4 * t, 4), AX.X).then_inc(squares, 1)

            out_evac_job(3)
            total_squares(8, out_sq)
            dve.wait_ge(x_again, 16)
            dve.wait_ge(out_evac, 8)
            for t in range(TT):
                dve.wait_ge(roots, 3 + t + 1)
                own.done(V.reciprocal(col(RS_X + t), col(RS_X + t)))
                for b in range(2):
                    c = slice(1024 * b, 1024 * b + 1024)
                    STT(out=xs[:, t, c], in0=y_mix[:, t, c], scalar=col(RS_X + t), in1=xs[:, t, c], op0=ALU.mult,
                        op1=ALU.add).then_inc(res_ready, 1)
                if t == 0:
                    split(Turn(UP_T + 1), 1)
                dve.wait_ge(res_sq, 2 * t + 2)
                V.reduce_sum(col(RS_1 + t), col(SS_1 + 2 * t, 2), AX.X).then_inc(squares, 1)
            for t in range(TT):
                dve.wait_ge(roots, 5 + t + 1)
                own.done(V.reciprocal(col(RS_1 + t), col(RS_1 + t)))
            for b in range(2):
                for t in range(TT):
                    c = slice(1024 * b, 1024 * b + 1024)
                    V.tensor_scalar(y_mix[:, t, c], xs[:, t, c], col(RS_1 + t), None, ALU.mult).then_inc(normed, 1)

            def tap(j, k):
                return convp[:, j, one(k)]

            def conv_unit(i, s, unit, banks, job):
                dve.wait_ge(u_low_ready, job * 2 + (unit + 1))
                b = banks + 2 * unit
                V.tensor_tensor(u_pad[:, :, 2:], ps[:, b:b + 2, 0:SEQ], u_low[:], ALU.add).then_inc(ffn_evac, 1)
                dve.wait_ge(ffn_evac, job * 2 + (unit + 1))
                took = job * 2 + unit
                if not isinstance(took, int) or took > 0:
                    dve.wait_ge(act_took_conv, took)
                k0 = i * 4 + (FF_TILES * s + 2 * unit)
                for v in range(2):
                    ins = V.tensor_scalar(conv[:, v, :], u_pad[:, v, 2:], tap(2, k0 + v), tap(3, k0 + v),
                                          ALU.mult, ALU.add)
                own.done(ins)
                for v in range(2):
                    ins = STT(out=conv[:, v, :], in0=u_pad[:, v, 1:SEQ + 1], scalar=tap(1, k0 + v),
                              in1=conv[:, v, :], op0=ALU.mult, op1=ALU.add)
                own.done(ins)
                for v in range(2):
                    ins = STT(out=conv[:, v, :], in0=u_pad[:, v, 0:SEQ], scalar=tap(0, k0 + v),
                              in1=conv[:, v, :], op0=ALU.mult, op1=ALU.add)
                if s == 0:
                    ins.then_inc(conv_ready, 1)
                else:
                    own.done(ins)
                    V.tensor_tensor(conv[:], conv[:], gate_act[:, k_tiles(i, unit), 1, :],
                                    ALU.mult).then_inc(conv_ready, 1)

            def ff_low(i, unit):
                dve.wait_ge(act_took_conv, i * 4 + (unit + 3))
                V.tensor_tensor(ffT[:, k_tiles(i, unit), 1, :], conv[:],
                                ffT[:, k_tiles(i, unit), 0, :].bitcast(F32), ALU.subtract).then_inc(ff_lo_ready, 1)

            def up_evac_dve(i, s, n):
                if n in (3, 5):
                    unit = (n - 3) // 2
                    if s == 1:
                        conv_unit(i, 0, unit, 0, i * 2)
                    else:
                        conv_unit(i - 1, 1, unit, 4, i * 2 - 1)
                if n in (4, 6) and s == 0:
                    ff_low(i - 1, (n - 4) // 2)

            def up_job(i, s, span, prev):
                for n in range(8):
                    if isinstance(i, int) and s == 0:
                        if n >= 4:
                            split(Turn(UP_T + n // 2), n % 2)
                        parts_low(h2T, n, KT + LAT_TILES, KT)
                    else:
                        split(Turn(UP_T + 4 * s + n // 2, 8, i, span), n % 2)
                    if prev:
                        up_evac_dve(i, s, n)

            up_job(0, 0, None, False)
            dve.wait_ge(consts, 5)
            up_job(0, 1, None, True)
            with dve.Fori(1, QUADS) as i:
                own.enter(i, 1, 10)
                for s in range(2):
                    up_job(i, s, range(1, QUADS), True)
            own.leave(QUADS - 1)

            def down_evac(j):
                dve.wait_ge(halves_used, halves_by(DOWN_T + 12 * j + 11))
                for t in range(TT):
                    if t == 1:
                        dve.wait_ge(down_sq, 2 * j + 1)
                    V.tensor_tensor(y_ffn[:, t, W * j:W * j + W], ps[:, 2 * (j % 2) + t, :],
                                    ffn_gain[:, W * j:W * j + W], ALU.mult).then_inc(ffn_evac, 1)

            for j in range(4):
                for n in range(2 * DOWN_CHUNKS):
                    split(Turn(DOWN_T + 12 * j + n // 2), n % 2)
                    if j == 0:
                        up_evac_dve(QUADS, 0, n)
                    elif n == 3:
                        if j == 1:
                            dve.wait_ge(ffn_gain_loaded, 16)
                        down_evac(j - 1)
            down_evac(3)
            total_squares(8, down_sq)
            for t in range(TT):
                dve.wait_ge(roots, 7 + t + 1)
                own.done(V.reciprocal(col(RS_X + t), col(RS_X + t)))
                for b in range(2):
                    y = y_ffn[:, t, 1024 * b:1024 * b + 1024]
                    STT(out=y, in0=y, scalar=col(RS_X + t), in1=xs[:, t, 1024 * b:1024 * b + 1024],
                        op0=ALU.mult, op1=ALU.add).then_inc(y_ready, 1)

        @block.tensor
        def _(pe):
            mm = nc.tensor.matmul

            def rows_half(turn, half, aT, k0, bank, start, stop, width=W, n=2):
                pe.wait_ge(lo_ready, turn.upto(half))
                slot = turn.half_slot(half)
                for kk in range(n):
                    for t in range(TT):
                        acc = ps[:, bank + t, 0:width]
                        ah, al = (aT[:, k0 + kk, v, P * t:P * t + P] for v in range(2))
                        mm(acc, ah, hi[:, slot, kk, 0:width], start=start and kk == 0, stop=False)
                        mm(acc, ah, lo[:, slot, kk, 0:width], start=False, stop=False)
                        last = mm(acc, al, hi[:, slot, kk, 0:width], start=False, stop=stop and kk == n - 1)
                last.then_inc(halves_used, 1)

            def turn_128(dst, src, rows=P):
                return nc.tensor.transpose(dst, src, ident[0:rows, 0:rows])

            pe.wait_ge(consts, 2)
            pe.wait_ge(gains_loaded, 64)
            turn_128(ps[:, 0, 0:38], gain_rows[:], 38).then_inc(columns_done, 1)

            def turn_tile(src, t, k):
                c = 256 * (k % 2) + P * t
                turn_128(ps[:, 4 + k // 2 % 4, c:c + P], src[:, t, P * k:P * k + P]).then_inc(turned, 1)

            for t in range(TT):
                pe.wait_ge(normed, t + 1)
                for k in range(8):
                    turn_tile(xs, t, k)

            def free_set(job):
                if job >= 2:
                    pe.wait_ge(mix_act, job - 1)
                    pe.wait_ge(mix_dve, job - 1)

            for j, width in enumerate((W, LAT_COLS - W)):
                for n in range(8):
                    if j == 0:
                        pe.wait_ge(parts_lo, 2 * n + 2)
                    if j == 0 and n == 0:
                        pe.wait_ge(columns_ready, 1)
                    rows_half(Turn(LAT_T + 4 * j + n // 2), n % 2, hT, 2 * n, 2 * j, n == 0, n == 7, width)
                    if j == 0 and n < 4:
                        for k in (8 + 2 * n, 9 + 2 * n):
                            for t in range(TT):
                                turn_tile(xs, t, k)
                    if j == 1 and n == 2:
                        pe.wait_ge(convs_loaded, 32)
                        for i in range(4):
                            last = turn_128(ps[:, 4, 88 * i:88 * i + 88], conv_rows[:, i, :], 88)
                        last.then_inc(columns_done, 1)
            for j in range(FV_BLOCKS):
                free_set(2 + j)
                for n in range(8):
                    rows_half(Turn(FV_T + 4 * j + n // 2), n % 2, hT, 2 * n, 2 * (j % 2), n == 0, n == 7, FV_W)
                    if j == 1 and n == 2:
                        pe.wait_ge(normed, 2 * TT)
                        pe.wait_ge(columns_ready, 2)
                        for k in range(LAT_TILES):
                            for t in range(TT):
                                c = 256 * (k % 2) + P * t
                                turn_128(ps[:, 4 + k // 2, c:c + P], lat_nat[:, t, P * k:P * k + P]).then_inc(turned, 1)
            pe.wait_ge(parts_lo, KT + LAT_TILES)
            for j in range(3):
                free_set(5 + j)
                for n in range(2):
                    rows_half(Turn(UQ_T + j), n, latT, 2 * n, 2 * ((5 + j) % 2), n == 0, n == 1)
            for j in range(4):
                free_set(8 + j)
                rows_half(Turn(UKV_T + j // 2), j % 2, latT, Q_LORA // P, 2 * (j % 2), True, True)

            def turn_item(r):
                if r >= 4:
                    pe.wait_ge(items_dve if r % 2 else items_act, (r - 4) // 2 + 1)
                bank = ps[:, 4 + r % 4, :]
                if r == 0:
                    pe.wait_ge(mix_act, 12)
                    pe.wait_ge(mix_dve, 12)
                if r == 4:
                    pe.wait_ge(kpe_roped, 2)
                if r == 5:
                    pe.wait_ge(q_roped, 2)
                if r == 11:
                    pe.wait_ge(forget_ready, 1)
                    pe.wait_ge(consts, 4)
                    f = [fgt[:, 3, t, :] for t in range(TT)]
                    tri, ones = tri_ones[:, 0:P], tri_ones[:, P:2 * P]
                    mm(bank[0:HEADS, 0:SEQ], f[0], tri_ones[:], start=True, stop=False)
                    mm(bank[0:HEADS, P:SEQ], f[1], tri, start=False, stop=True)
                    mm(bank[:, SEQ:SEQ + HEADS], tri, f[0], start=True, stop=True)
                    mm(bank[:, SEQ + HEADS:SEQ + 2 * HEADS], ones, f[0], start=True, stop=False)
                    mm(bank[:, SEQ + HEADS:SEQ + 2 * HEADS], tri, f[1], start=False, stop=True)\
                        .then_inc(items_turned, 1)
                    return
                for v in range(1 if r == 4 else 2):
                    for t in range(TT):
                        c = 256 * v + P * t
                        if r < 4:
                            src = k_nat[:, t, 2 * r + v, :]
                        elif r == 4:
                            src = kpe_nat[:, t].rearrange("p a d -> p (a d)")
                        elif r < 9:
                            src = q_nat[:, t, 2 * (r - 5) + v, 0:HD]
                        else:
                            h = 4 * (r - 9) + 2 * v
                            src = qpe_nat[:, t, h:h + 2, :].rearrange("p a d -> p (a d)")
                        last = turn_128(bank[:, c:c + P], src)
                last.then_inc(items_turned, 1)

            for j in range(4):
                free_set(12 + j)
                for n in range(8):
                    turn = Turn(FQK_T + 4 * j + n // 2)
                    pe.wait_ge(lo_ready, turn.upto(n % 2))
                    slot = turn.half_slot(n % 2)
                    for kk in range(2):
                        for f in range(4):
                            acc = ps[:, 2 * (j % 2) + f // 2, 256 * (f % 2):256 * (f % 2) + 256]
                            k = 2 * n + kk
                            first, final = n == 0 and kk == 0 and f % 2 == 0, n == 7 and kk == 1
                            wc = slice(P * f, P * f + P)
                            mm(acc, hi[:, slot, kk, wc], hT[:, k, 0, :], start=first, stop=False, skip_group_check=True)
                            mm(acc, hi[:, slot, kk, wc], hT[:, k, 1, :], start=False, stop=False, skip_group_check=True)
                            last = mm(acc, lo[:, slot, kk, wc], hT[:, k, 0, :], start=False, stop=final,
                                      skip_group_check=True)
                    last.then_inc(halves_used, 1)
                    if (8 * j + n) % 2 == 0 and (8 * j + n) // 2 < 12:
                        turn_item((8 * j + n) // 2)

            def scores(h, par):
                pe.wait_ge(q_staged, h + 1)
                if not isinstance(h, int) or h > 0:
                    pe.wait_ge(heads_hi, h * 2)
                    pe.wait_ge(heads_lo, h * 2)
                half = slice(64 * par, 64 * par + 64)
                for q in range(TT):
                    keys = P * (q + 1)
                    c, qs = P * q, slice(P * q, P * q + P)
                    acc = ps[:, 4, c:c + keys]
                    mm(acc, q_now[:, 0, qs], head(qkT, h, 1, keys), start=True, stop=False)
                    mm(acc, qpe_now[half, qs], kpeT[half, 0:keys], start=False, stop=False)
                    mm(ps[:, 4, c + keys - P:c + keys], ident[:], mask_mla[:], start=False, stop=True)
                for q in range(TT):
                    keys = P * (q + 1)
                    c, qs = P * q, slice(P * q, P * q + P)
                    acc = ps[:, 5, c:c + keys]
                    mm(acc, q_now[:, 1, qs], head(fqkT, h, 1, keys), start=True, stop=False)
                    mm(acc, head_row[:], negc[:, 0:keys], start=False, stop=False)
                    last = mm(ps[:, 5, c + keys - P:c + keys], ident[:], mask_fox[:], start=False, stop=True)
                last.then_inc(scores_done, 1)

            def head(t, h, which, n):
                return t[:, one(h), which, 0:n].rearrange("p a q -> p (a q)")

            def turn_probs(h):
                pe.wait_ge(probs_ready, h + 1)
                if not isinstance(h, int) or h > 0:
                    pe.wait_ge(probsT_act, h)
                    pe.wait_ge(probsT_dve, h)
                for b in range(2):
                    for c in range(3):
                        last = turn_128(ps[:, 6 + b, P * c:P * c + P], probs[:, b, P * c:P * c + P])
                last.then_inc(probs_turned, 1)

            def outputs(h):
                pe.wait_ge(v_staged, h + 1)
                pe.wait_ge(probsT_act, h + 1)
                pe.wait_ge(probsT_dve, h + 1)
                for b in range(2):
                    mm(ps[:, 4 + b, 0:SEQ], v_now[:, b, 0, :], probsT[:, b, 0:SEQ], start=True, stop=False)
                    last = mm(ps[:, 4 + b, P:SEQ], v_now[:, b, 1, :], probsT[:, b, SEQ:SEQ + P], start=False, stop=True)
                last.then_inc(heads_done, 1)

            def gate_job(p, s, span):
                h = p * 2 + s
                if isinstance(p, int):
                    free_set(16 + s)
                else:
                    pe.wait_ge(gate_sum, h * 2 - 2)
                scores(h, s)
                for n in range(8):
                    rows_half(Turn(GATES_T + 4 * s + n // 2, 8, p, span), n % 2, hT, 2 * n, 2 * s, n == 0, n == 7)
                    if n == 3:
                        turn_probs(h)
                    if n == 5:
                        outputs(h)

            gate_job(0, 0, None)
            gate_job(0, 1, None)
            with pe.Fori(1, 4) as p:
                for s in range(2):
                    gate_job(p, s, range(1, 4))

            def turn_merged(c):
                pe.wait_ge(merged_ready, c + 1)
                for u in range(2):
                    if 2 * c + u >= 4:
                        pe.wait_ge(merged_lo, 2 * c + u - 3)
                    for v in range(2):
                        for t in range(TT):
                            f = P * (2 * u + v)
                            last = turn_128(ps[:, 4 + (2 * c + u) % 4, 256 * v + P * t:256 * v + P * t + P],
                                            m_fox[:, t, f:f + P])
                    last.then_inc(merged_turned, 1)

            for c in range(4):
                for b, oT in enumerate((o_mlaT, o_foxT)):
                    if c == 0:
                        pe.wait_ge(gate_sum, 14 + 2 * b)
                        if b == 0:
                            pe.wait_ge(heads_lo, 2 * HEADS)
                            pe.wait_ge(heads_hi, 2 * HEADS)
                    else:
                        pe.wait_ge(branch_evac, 2 * (2 * c + b - 1))
                    for n in range(4):
                        rows_half(Turn(BRANCH_T + 4 * c + 2 * b + n // 2), n % 2, oT, 2 * n, 2 * b, n == 0, n == 3)
                        if b == 0 and n == 2 and c > 0:
                            turn_merged(c - 1)
            for j in range(4):
                if j < 2:
                    pe.wait_ge(branch_evac, 14 + 2 * j)
                else:
                    pe.wait_ge(out_evac, 2 * (j - 1))
                    pe.wait_ge(out_sq, 2 * (j - 1))
                for n in range(8):
                    if j == 0 and n % 2 == 0:
                        pe.wait_ge(merged_lo, n + 2)
                    rows_half(Turn(OUT_T + 4 * j + n // 2), n % 2, mergedT, 2 * n, 2 * (j % 2), n == 0, n == 7)
                    if j == 0 and n == 2:
                        turn_merged(3)
            pe.wait_ge(out_evac, 8)
            pe.wait_ge(out_sq, 8)
            for t in range(TT):
                pe.wait_ge(normed, 2 * TT + t + 1)
                for k in range(8):
                    turn_tile(y_mix, t, k)

            def up_half(turn, n, bank):
                pe.wait_ge(lo_ready, turn.upto(n % 2))
                slot = turn.half_slot(n % 2)
                for kk in range(2):
                    k = 2 * n + kk
                    for f in range(4):
                        wc = slice(P * f, P * f + P)
                        mm(ps[:, bank + f, :], hi[:, slot, kk, wc], h2T[:, k, :, :].rearrange("p a q -> p (a q)"),
                           start=k == 0, stop=False)
                        last = mm(ps[:, bank + f, 0:SEQ], lo[:, slot, kk, wc], h2T[:, k, 0, :],
                                  start=False, stop=k == KT - 1)
                last.then_inc(halves_used, 1)

            def up_job(i, s, span):
                if not isinstance(i, int):
                    pe.wait_ge(ffn_evac, i * 4 + (2 * s - 2))
                for n in range(8):
                    if isinstance(i, int) and s == 0:
                        pe.wait_ge(parts_lo, KT + LAT_TILES + 2 * n + 2)
                    up_half(Turn(UP_T + 4 * s + n // 2, 8, i, span), n, 4 * s)
                    if isinstance(i, int) and s == 0 and n < 4:
                        pe.wait_ge(normed, 4 * TT)
                        for k in (8 + 2 * n, 9 + 2 * n):
                            for t in range(TT):
                                turn_tile(y_mix, t, k)

            up_job(0, 0, None)
            up_job(0, 1, None)
            with pe.Fori(1, QUADS) as i:
                for s in range(2):
                    up_job(i, s, range(1, QUADS))
            with pe.Fori(0, 2) as p:
                for s in range(2):
                    pe.wait_ge(ffn_evac, p * 4 + (4 * QUADS - 2 + 2 * s))
                    if s == 0:
                        pe.wait_ge(ff_lo_ready, 2 * (QUADS - 1))
                    for n in range(2 * DOWN_CHUNKS):
                        if n == 2 * DOWN_CHUNKS - 2:
                            pe.wait_ge(ff_lo_ready, 2 * QUADS)
                        rows_half(Turn(DOWN_T + 12 * s + n // 2, 24, p, range(2)), n % 2, ffT, 2 * n, 2 * s,
                                  n == 0, n == 2 * DOWN_CHUNKS - 1)


_INS = ["x", "positions", "pre_mix_norm", "w_in", "q_a_norm", "w_uq", "kv_a_norm", "w_ukv", "b_forget", "b_gate",
        "w_branch_mla", "w_branch_fox", "w_out", "post_mix_norm", "pre_ffn_norm", "w_up", "conv_w", "conv_b",
        "w_down", "post_ffn_norm"]


def kernel(**inputs):
    import numpy as _np
    import concourse.bacc as _bacc
    from concourse import mybir as _mybir
    from concourse.bass_utils import run_bass_kernel_spmd as _run

    nc = _bacc.Bacc("TRN2", target_bir_lowering=False, num_devices=1)
    arrays, args = {}, []
    freq = (1.0 / 10000.0 ** (_np.arange(0, ROPE, 2, dtype=_np.float32) / ROPE)).astype(_np.float32)[None, :]
    for name, a in [(n, _np.ascontiguousarray(inputs[n])) for n in _INS] + [("rope_freq", freq)]:
        arrays[f"in_{name}_dram"] = a
        args.append(nc.dram_tensor(f"in_{name}_dram", a.shape, _mybir.dt.from_np(a.dtype), kind="ExternalInput").ap())
    args.append(nc.dram_tensor("out_dram", (1, SEQ, D), F32, kind="ExternalOutput").ap())
    residual_block(nc, *args)
    r = _run(nc, [arrays], core_ids=[0])
    return r.results[0]["out_dram"]
```

```python
import math
from contextlib import ExitStack

import concourse.bass as bass
from concourse import mybir

F32 = mybir.dt.float32
F32R = mybir.dt.float32r
I32 = mybir.dt.int32
BF16 = mybir.dt.bfloat16
ACT = mybir.ActivationFunctionType
ALU = mybir.AluOpType
AX = mybir.AxisListType

P = 128
SEQ, D = 256, 2048
TT = SEQ // P
Q_LORA, KV_LORA, ROPE = 512, 256, 64
HEADS, HD = 8, 128
QH = HD + ROPE
D_FF = 5632
LAT_COLS = Q_LORA + KV_LORA + ROPE
FOX0 = LAT_COLS
FV0 = FOX0 + 2 * HEADS * HD
GATE0 = FV0 + HEADS * HD + HEADS
FV_COLS = HEADS * HD + HEADS
FV_BLOCKS = 3
FV_W = FV_COLS // FV_BLOCKS
EPS = 1e-6
SCALE_MLA = float(QH) ** -0.5
SCALE_FOX = float(HD) ** -0.5
HIDDEN_SCORE = -1e30
MLA_CHUNK = 64
DECAY_ROWS = 64 + HEADS

KT = D // P
FF_TILES = D_FF // P
W = 512
KC = 4
QUADS = FF_TILES // 4
DOWN_CHUNKS = FF_TILES // KC
LAT_TILES = (Q_LORA + KV_LORA) // P

LAT_T = 0
FV_T = LAT_T + 8
UQ_T = FV_T + 4 * FV_BLOCKS
UKV_T = UQ_T + 3
FQK_T = UKV_T + 2
GATES_T = FQK_T + 16
BRANCH_T = GATES_T + 32
OUT_T = BRANCH_T + 16
UP_T = OUT_T + 16
DOWN_T = UP_T + 8 * QUADS
END_T = DOWN_T + 4 * 12
HALVES = [2] * END_T
for _t in (DOWN_T + 22, DOWN_T + 23, DOWN_T + 46, DOWN_T + 47):
    HALVES[_t] = 0
BEFORE = [0]
for _h in HALVES:
    BEFORE.append(BEFORE[-1] + _h)


def halves_by(turn, half=2):
    if turn < 0:
        return 0
    return BEFORE[turn] + min(half, HALVES[turn])


def down_turn(j):
    return DOWN_T + 24 * (j // 2) + DOWN_CHUNKS * (j % 2)


def turn_before(turn, ring):
    turn -= ring
    while turn >= 0 and HALVES[turn] == 0:
        turn -= ring
    return turn


def loads_by(turn):
    return sum(1 for t in range(turn % 4, turn + 1, 4) if HALVES[t])


class Turn:

    def __init__(self, first, per=0, i=0, span=None):
        self.first, self.per, self.i, self.span = first, per, i, span

    def plus(self, n):
        return Turn(self.first + n, self.per, self.i, self.span)

    def value(self, f):
        if isinstance(self.i, int):
            return f(self.first + self.per * self.i)
        v = [f(self.first + self.per * k) for k in self.span]
        step = v[-1] - v[-2]
        return self.i * step + max(x - step * k for x, k in zip(v, self.span))

    def slot(self):
        return self.first % 4

    def half_slot(self, half):
        return (2 * self.first + half) % 4

    def loaded(self):
        return self.value(lambda t: 16 * loads_by(t))

    def upto(self, half):
        return self.value(lambda t: halves_by(t, half + 1))

    def slot_freed(self):
        return self.value(lambda t: halves_by(turn_before(t, 4)))

    def half_freed(self, half):
        return self.value(lambda t: halves_by(turn_before(t, 2), half + 1))


class Own:

    def __init__(self, eng, sem):
        self.eng, self.sem, self.n, self.i, self.a, self.per = eng, sem, 0, None, 0, 0

    def enter(self, i, a, per):
        self.i, self.a, self.per, self.start = i, a, per, self.n

    def leave(self, count):
        assert self.n - self.start == self.per, (self.n - self.start, self.per)
        self.n = self.start + self.per * count
        self.i = None

    def done(self, ins):
        ins.then_inc(self.sem, 1)
        self.n += 1
        if self.i is None:
            self.eng.wait_ge(self.sem, self.n)
        else:
            self.eng.wait_ge(self.sem, self.i * self.per + (self.n - self.a * self.per))


def residual_block(nc, x, positions, pre_mix_norm, w_in, q_a_norm, w_uq, kv_a_norm, w_ukv, b_forget,
                   b_gate, w_branch_mla, w_branch_fox, w_out, post_mix_norm, pre_ffn_norm, w_up,
                   conv_w, conv_b, w_down, post_ffn_norm, inv_freq, out):
    ctx = ExitStack()
    with ctx:
        def at(name, shape, dt, offset):
            return nc.alloc_sbuf_tensor_at(name, shape, dt, offset=offset)

        def sem(name):
            return ctx.enter_context(nc.semaphore(name))

        KB = 1024
        base = 16512
        raw = at("raw", [P, 4, KC, W], F32, base)
        hi = at("hi", [P, 4, 2, W], F32R, base + 32 * KB)
        lo = at("lo", [P, 4, 2, W], F32R, base + 48 * KB)
        body = base + 64 * KB
        xs = at("xs", [P, TT, D], F32, body)
        lat_nat = at("lat_nat", [P, TT, LAT_COLS], F32, body)
        rope_tmp = at("rope_tmp", [P, 4, TT, HEADS, ROPE // 2], F32, body + 7 * KB)
        probs = at("probs", [P, 2, 384], F32, body)
        probsT = at("probsT", [P, 2, 384], F32, body + 3 * KB)
        q_now = at("q_now", [P, 2, SEQ], F32, body + 6 * KB)
        qpe_now = at("qpe_now", [P, SEQ], F32, body + 8 * KB)
        v_now = at("v_now", [P, 2, TT, HD], F32, body + 9 * KB)
        head_rows = at("head_rows", [DECAY_ROWS, P], BF16, body + 11 * KB)
        head_of_row = at("head_of_row", [DECAY_ROWS, HEADS], BF16, body + 11 * KB + 256)
        decay_parts = at("decay_parts", [DECAY_ROWS, SEQ], BF16, body + 11 * KB + 288)
        B = body + 16 * KB
        hT = at("hT", [P, KT, 2, SEQ], F32R, B)
        mergedT = at("mergedT", [P, KT, 2, SEQ], F32R, B)
        h2T = at("h2T", [P, KT, 2, SEQ], F32R, B)
        y_ffn = at("y_ffn", [P, TT, D], F32, B)
        ffn_gain = at("ffn_gain", [P, D], F32, B + 16 * KB)
        ffn_junk = at("ffn_junk", [P, 2 * W], F32, B + 24 * KB)
        C = B + 32 * KB
        fqkT = at("fqkT", [P, HEADS, 2, SEQ], F32, C)
        o_foxT = at("o_foxT", [P, HEADS, 2, SEQ], F32R, C)
        vf = at("vf", [P, TT, FV_COLS], F32, C + 16 * KB)
        m_mla = at("m_mla", [P, TT, W], F32, C + 16 * KB)
        m_fox = at("m_fox", [P, TT, W], F32, C + 20 * KB)
        E = C + 16 * KB + 8448
        qkT = at("qkT", [P, HEADS, 2, SEQ], F32, E)
        o_mlaT = at("o_mlaT", [P, HEADS, 2, SEQ], F32R, E)
        qpeT = at("qpeT", [P, HEADS // 2, SEQ], F32, E + 16 * KB)
        kpeT = at("kpeT", [P, SEQ], F32, E + 20 * KB)
        v_mla = at("v_mla", [P, TT, HEADS, HD], F32, E + 21 * KB)
        mix_gain = at("mix_gain", [P, D], F32, E + 21 * KB)
        G = E + 29 * KB
        q_nat = at("q_nat", [P, TT, HEADS, QH], F32, G)
        k_nat = at("k_nat", [P, TT, HEADS, HD], F32, G + 12 * KB)
        latT = at("latT", [P, LAT_TILES, 2, SEQ], F32R, G + 20 * KB)
        gates = at("gates", [P, TT, 2 * D], F32, G)
        y_mix = at("y_mix", [P, TT, D], F32, G)
        junk = at("junk", [P, D], F32, G + 16 * KB)
        sum_junk = at("sum_junk", [P, D], F32, G + 24 * KB)
        tri_ones = at("tri_ones", [P, 2 * P], F32, G + 32 * KB)
        ffT = at("ffT", [P, FF_TILES, 2, SEQ], F32R, C)
        gate_act = at("gate_act", [P, FF_TILES, 2, SEQ], F32, C)
        J = body + 136 * KB
        assert G + 33 * KB <= J and C + 88 * KB <= J
        convp = at("convp", [P, 4, 2 * FF_TILES], F32, J)
        gcol = at("gcol", [P, 48], F32, J + 1408)
        small = at("small", [P, 64], F32, J + 1600)
        J2 = J + 1856
        ident = at("ident", [P, P], F32, J2)
        ident_bf = at("ident_bf", [P, P], BF16, J2 + 512)
        mask_fox = at("mask_fox", [P, P], BF16, J2 + 768)
        mask_mla = at("mask_mla", [P, P], BF16, J2 + 1024)
        bgate = at("bgate", [P, 2, W], F32, J2 + 1536)
        qpe_nat = at("qpe_nat", [P, TT, HEADS, ROPE], F32, J2 + 1536)
        sc_end = J2 + 1536 + 4096
        kpe_nat = at("kpe_nat", [P, TT, 2, ROPE], F32, body + 15 * KB)
        gain_rows = at("gain_rows", [38, P], F32, E)
        conv_rows = at("conv_rows", [88, 4, P], F32, E + 512)
        angle = at("angle", [P, 6, TT, ROPE // 2], F32, E + 3 * KB)
        inv_sb = at("inv_sb", [P, ROPE // 2], F32, E + 5 * KB)
        pos_i = at("pos_i", [P, TT], I32, E + 5 * KB + 128)
        fgt = at("fgt", [P, 4, TT, HEADS], F32, G + 34 * KB)
        negc = at("negc", [DECAY_ROWS, SEQ], F32, body + 12 * KB)
        log_forget = at("log_forget", [P, TT, DECAY_ROWS], F32, body + 14 * KB)
        cossin = at("cossin", [P, 2, TT, ROPE // 2], F32, G + 33 * KB)
        bfor = at("bfor", [P, HEADS], F32, G + 34 * KB + 256)
        u_low = at("u_low", [P, 2, SEQ], F32, J2)
        u_pad = at("u_pad", [P, 2, SEQ + 2], F32, J2 + 2048)
        conv = at("conv", [P, 2, SEQ], F32, J2 + 4128)
        assert max(sc_end, J2 + 4128 + 2048) <= 229344 and G + 34 * KB + 320 <= J, (sc_end, G + 34 * KB + 320, J)

        EPS_C, ONE_C, SS_X, RS_X, SS_L, RS_L = 0, 1, 2, 4, 6, 10
        MX, NB, SUM, CQ, SS_O, RS_1, SS_1 = 14, 18, 22, 26, 42, 50, 56

        def col(c, n=1):
            return small[:, c:c + n]

        ps = ctx.enter_context(nc.psum_tensor("ps", [P, 8, 512], F32))

        chunk_loaded = [sem(f"chunk_loaded_{i}") for i in range(4)]
        hi_ready = sem("hi_ready")
        lo_ready = sem("lo_ready")
        halves_used = sem("halves_used")
        x_loaded = [sem(f"x_loaded_{t}_{b}") for t in range(TT) for b in range(2)]
        gains_loaded, convs_loaded, rope_loaded = sem("gains_loaded"), sem("convs_loaded"), sem("rope_loaded")
        bfor_loaded = sem("bfor_loaded")
        bgate_loaded = [sem(f"bgate_loaded_{i}") for i in range(2)]
        mix_gain_loaded, x_again, ffn_gain_loaded = sem("mix_gain_loaded"), sem("x_again"), sem("ffn_gain_loaded")
        out_stored = sem("out_stored")
        consts = sem("consts")
        act_own, dve_own, pool_own = sem("act_own"), sem("dve_own"), sem("pool_own")
        squares = sem("squares")
        roots = sem("roots")
        normed = sem("normed")
        columns_done, columns_ready = sem("columns_done"), sem("columns_ready")
        angles_ready, sines_ready = sem("angles_ready"), sem("sines_ready")
        turned = sem("turned")
        parts_hi, parts_lo = sem("parts_hi"), sem("parts_lo")
        mix_act, mix_dve = sem("mix_act"), sem("mix_dve")
        q_roped, kpe_roped = sem("q_roped"), sem("kpe_roped")
        items_turned, items_act, items_dve = sem("items_turned"), sem("items_act"), sem("items_dve")
        forget_abs, forget_soft, forget_ready, decay_summed, decay_ready = (
            sem("forget_abs"), sem("forget_soft"), sem("forget_ready"), sem("decay_summed"), sem("decay_ready"))
        q_staged, v_staged = sem("q_staged"), sem("v_staged")
        scores_done, shifts_ready, probs_raw, probs_ready = (
            sem("scores_done"), sem("shifts_ready"), sem("probs_raw"), sem("probs_ready"))
        probs_turned, probsT_act, probsT_dve = sem("probs_turned"), sem("probsT_act"), sem("probsT_dve")
        heads_done, heads_hi, heads_lo = sem("heads_done"), sem("heads_hi"), sem("heads_lo")
        gate_sum, gates_ready = sem("gate_sum"), sem("gates_ready")
        merged_ready, merged_turned, merged_hi, merged_lo = (
            sem("merged_ready"), sem("merged_turned"), sem("merged_hi"), sem("merged_lo"))
        out_sq, out_evac = sem("out_sq"), sem("out_evac")
        res_ready, res_sq = sem("res_ready"), sem("res_sq")
        u_low_ready, ffn_evac, conv_ready = sem("u_low_ready"), sem("ffn_evac"), sem("conv_ready")
        branch_evac = sem("branch_evac")
        act_took_conv, ff_lo_ready = sem("act_took_conv"), sem("ff_lo_ready")
        down_sq = sem("down_sq")
        tile0_summed = sem("tile0_summed")
        tile0_scale, tile0_normed = sem("tile0_scale"), sem("tile0_normed")
        first_half_loaded = sem("first_half_loaded")
        y_ready = sem("y_ready")

        block = ctx.enter_context(nc.Block())

        def k_view(w):
            return w.rearrange("(k p) c -> p k c", p=P)

        w_in_v, w_uq_v, w_ukv_v = k_view(w_in), k_view(w_uq), k_view(w_ukv)
        wbm_v, wbf_v, w_out_v = k_view(w_branch_mla), k_view(w_branch_fox), k_view(w_out)
        w_up_v, w_down_v = k_view(w_up), k_view(w_down)
        x_v = x[0].rearrange("(t p) d -> p t d", p=P)
        out_v = out[0].rearrange("(t p) d -> p t d", p=P)
        bgate_v = b_gate.rearrange("(a n) -> a n", a=1)

        def half_row(b):
            return slice(D // 2 * b, D // 2 * b + D // 2)

        def cols(w):
            return bass.ds(w, W) if not isinstance(w, int) else slice(w, w + W)

        def wide(turn):
            return raw[:, turn.slot(), :, :].rearrange("p (k b) c -> p k (b c)", k=2)

        def raw_half(turn, half, width, wide_chunk):
            if wide_chunk:
                return wide(turn)[:, :, W * half:W * half + W]
            return raw[:, turn.slot(), 2 * half:2 * half + 2, 0:width]

        def cos_sin(j):
            return cossin[:, j]

        def q_flat(t, j):
            return q_nat[:, t].rearrange("p h d -> p (h d)")[:, W * j:W * j + W]

        def heads_in_bank(bank):
            return ps[:, bank, :].rearrange("p (h d) -> p h d", h=2)

        def kv_bank(b):
            v = ps[:, b, :].rearrange("p (h d) -> p h d", h=2)
            return v[:, :, 0:HD], v[:, :, HD:2 * HD]

        def item_from(r):
            bank = ps[:, 4 + r % 4, :]
            return bank[:, 0:SEQ] if r == 4 else bank.rearrange("p (h q) -> p h q", h=2)

        def item_to(r):
            if r < 4:
                return qkT[:, 2 * r:2 * r + 2, 1, :]
            if r == 4:
                return kpeT[:]
            if r < 9:
                return qkT[:, 2 * (r - 5):2 * (r - 5) + 2, 0, :]
            return qpeT[:, 2 * (r - 9):2 * (r - 9) + 2, :]

        def fqk_to(j, b):
            h = 4 * (j % 2) + 2 * b
            return fqkT[:, h:h + 2, j // 2, :]

        def k_tiles(i, unit):
            k = i * 4 + 2 * unit
            return slice(k, k + 2) if isinstance(k, int) else bass.ds(k, 2)

        def one(h):
            return slice(h, h + 1) if isinstance(h, int) else bass.ds(h, 1)

        def span_of(c, n):
            return slice(c, c + n) if isinstance(c, int) else bass.ds(c, n)

        @block.sync
        def _(sp):
            def load(turn, src, n=KC, width=W):
                freed = turn.slot_freed()
                if not isinstance(freed, int) or freed > 0:
                    sp.wait_ge(lo_ready, freed)
                dst = raw[:, turn.slot(), 0:n, 0:width] if width <= W else wide(turn)
                sp.dma_start(dst, src).then_inc(chunk_loaded[turn.slot()], 16)

            def snap(c):
                return c if isinstance(c, int) else sp.snap(c)

            for t in range(TT):
                for b in range(2):
                    sp.dma_start(xs[:, t, half_row(b)], x_v[:, t, half_row(b)]).then_inc(x_loaded[2 * t + b], 16)
            for r0, gain in ((0, pre_mix_norm), (KT, pre_ffn_norm), (32, q_a_norm), (36, kv_a_norm)):
                rows = gain.shape[0] // P
                sp.dma_start(gain_rows[r0:r0 + rows, :], gain.rearrange("(r c) -> r c", c=P))\
                  .then_inc(gains_loaded, 16)
            sp.dma_start(raw[:, 0, 0:2, :], w_in_v[:, 0:2, 0:W]).then_inc(first_half_loaded, 16)
            sp.dma_start(raw[:, 0, 2:4, :], w_in_v[:, 2:4, 0:W]).then_inc(chunk_loaded[0], 16)
            for j, (c0, width) in enumerate(((0, W), (W, LAT_COLS - W))):
                for c in range(1 if j == 0 else 0, 4):
                    load(Turn(LAT_T + 4 * j + c), w_in_v[:, 4 * c:4 * c + 4, c0:c0 + width], KC, width)
                if j == 0:
                    with nc.allow_non_contiguous_dma(reason="256 positions"):
                        sp.dma_start(pos_i[:], positions.rearrange("b (t p) -> p (b t)", p=P))\
                          .then_inc(rope_loaded, 16)
                    sp.dma_start(inv_sb[:], inv_freq.to_broadcast([P, ROPE // 2])).then_inc(rope_loaded, 16)
                    sp.dma_start(bfor[:], b_forget.rearrange("(a n) -> a n", a=1).to_broadcast([P, HEADS]))\
                      .then_inc(bfor_loaded, 16)
                    sp.dma_start(conv_rows[:, 0:3, :], conv_w.rearrange("j (r c) -> r j c", c=P))\
                      .then_inc(convs_loaded, 16)
                    sp.dma_start(conv_rows[:, 3, :], conv_b.rearrange("(r c) -> r c", c=P)).then_inc(convs_loaded, 16)
            for j in range(FV_BLOCKS):
                for c in range(4):
                    c0 = FV0 + FV_W * j
                    load(Turn(FV_T + 4 * j + c), w_in_v[:, 4 * c:4 * c + 4, c0:c0 + FV_W], KC, FV_W)
            for j in range(3):
                load(Turn(UQ_T + j), w_uq_v[:, :, W * j:W * j + W])
            for j in range(2):
                load(Turn(UKV_T + j), w_ukv_v[:, :, 2 * W * j:2 * W * j + 2 * W], 2, 2 * W)
            for j in range(4):
                for c in range(4):
                    c0 = FOX0 + W * j
                    load(Turn(FQK_T + 4 * j + c), w_in_v[:, 4 * c:4 * c + 4, c0:c0 + W])

            def gate_loads(p, span):
                for s in range(2):
                    if not isinstance(p, int):
                        sp.wait_ge(gate_sum, p * 4 + (2 * s - 2))
                    else:
                        sp.wait_ge(items_turned, 11)
                    sp.dma_start(bgate[:, s, :], bgate_v[:, cols(p * (2 * W) + W * s)].to_broadcast([P, W]))\
                      .then_inc(bgate_loaded[s], 16)
                    for c in range(4):
                        load(Turn(GATES_T + 4 * s + c, 8, p, span),
                             w_in_v[:, 4 * c:4 * c + 4, cols(snap(p * (2 * W) + (GATE0 + W * s)))])

            gate_loads(0, None)
            with sp.Fori(1, 4) as p:
                gate_loads(p, range(1, 4))
            for c in range(4):
                for b, wv in enumerate((wbm_v, wbf_v)):
                    for k in range(2):
                        load(Turn(BRANCH_T + 4 * c + 2 * b + k), wv[:, 4 * k:4 * k + 4, W * c:W * c + W])
            for j in range(4):
                for c in range(4):
                    load(Turn(OUT_T + 4 * j + c), w_out_v[:, 4 * c:4 * c + 4, W * j:W * j + W])
                if j == 0:
                    sp.wait_ge(heads_lo, 2 * HEADS)
                    sp.wait_ge(heads_hi, 2 * HEADS)
                    sp.dma_start(mix_gain[:], post_mix_norm.rearrange("(a n) -> a n", a=1).to_broadcast([P, D]))\
                      .then_inc(mix_gain_loaded, 16)
                    sp.dma_start(xs[:], x_v).then_inc(x_again, 16)

            def up_loads(i, span):
                for s in range(2):
                    for c in range(4):
                        load(Turn(UP_T + 4 * s + c, 8, i, span),
                             w_up_v[:, 4 * c:4 * c + 4, cols(snap(i * W + D_FF * s))])

            up_loads(0, None)
            with sp.Fori(1, QUADS) as i:
                up_loads(i, range(1, QUADS))
            with sp.Fori(0, 2) as p:
                for s in range(2):
                    for c in range(DOWN_CHUNKS):
                        load(Turn(down_turn(s) + c, 24, p, range(2)),
                             w_down_v[:, 4 * c:4 * c + 4, cols(snap(p * (2 * W) + W * s))])
            for t in range(TT):
                for b in range(4):
                    sp.wait_ge(y_ready, 4 * t + b + 1)
                    sp.dma_start(out_v[:, t, W * b:W * b + W], y_ffn[:, t, W * b:W * b + W]).then_inc(out_stored, 16)
            sp.wait_ge(out_stored, 16 * 4 * TT)

        @block.gpsimd
        def _(pool):
            own = Own(pool, pool_own)
            own.done(pool.memset(col(ONE_C), 1.0))
            pool.memset(col(EPS_C), EPS).then_inc(consts, 1)
            pool.wait_ge(consts, 1)
            own.done(pool.memset(ident[:], 0.0))
            pool.affine_select(out=ident[:], in_=ident[:], compare_op=ALU.not_equal, fill=1.0, base=0,
                               pattern=[[-1, P]], channel_multiplier=1).then_inc(consts, 1)
            pool.wait_ge(consts, 2)
            own.done(pool.memset(tri_ones[:], 1.0))
            own.done(pool.memset(mask_fox[:], 0.0))
            own.done(pool.memset(mask_mla[:], 0.0))
            own.done(pool.memset(mask_mla[0:MLA_CHUNK, MLA_CHUNK:P], HIDDEN_SCORE / SCALE_MLA))
            pool.affine_select(out=tri_ones[:, 0:P], in_=tri_ones[:, 0:P], compare_op=ALU.is_ge, fill=0.0,
                               base=0, pattern=[[1, P]], channel_multiplier=-1).then_inc(consts, 1)
            pool.affine_select(out=mask_fox[:], in_=mask_fox[:], compare_op=ALU.is_ge,
                               fill=HIDDEN_SCORE / SCALE_FOX, base=0, pattern=[[-1, P]],
                               channel_multiplier=1).then_inc(consts, 1)
            pool.tensor_copy(ident_bf[:], ident[:]).then_inc(consts, 1)

            def stage(h, p, par):
                if not isinstance(h, int) or h > 0:
                    pool.wait_ge(scores_done, h)
                own.done(pool.tensor_copy(q_now[:, 0, :], qkT[:, h, 0, :]))
                own.done(pool.tensor_copy(q_now[:, 1, :], fqkT[:, h, 0, :]))
                half = slice(64 * par, 64 * par + 64)
                own.done(pool.tensor_copy(qpe_now[half, :], qpeT[half, one(p), :].rearrange("a b q -> a (b q)")))
                own.done(pool.tensor_copy(head_rows[:], head_of_row[:, one(h)].to_broadcast([DECAY_ROWS, P])))
                pool.sem_inc(q_staged, 1)
                if not isinstance(h, int) or h > 0:
                    pool.wait_ge(heads_done, h)
                own.done(pool.tensor_copy(v_now[:, 0, :, :], v_mla[:, :, h, :]))
                own.done(pool.tensor_copy(v_now[:, 1, :, :], vf[:, :, span_of(h * HD, HD)]))
                pool.sem_inc(v_staged, 1)

            pool.wait_ge(mix_act, 15)
            pool.wait_ge(mix_dve, 15)
            pool.wait_ge(items_act, 6)
            pool.wait_ge(items_dve, 5)
            pool.wait_ge(decay_ready, 2)
            for s in range(2):
                stage(s, 0, s)
            pool.wait_ge(mix_act, 16)
            pool.wait_ge(mix_dve, 16)
            with pool.Fori(1, 4) as p:
                own.enter(p, 1, 12)
                for s in range(2):
                    stage(p * 2 + s, p, s)
            own.leave(3)
            pool.wait_ge(turned, 4 * KT + 2 * LAT_TILES)
            pool.memset(u_pad[:, :, 0:2], 0.0).then_inc(consts, 1)
            pool.wait_ge(halves_used, halves_by(DOWN_T - 1))
            pool.dma_start(ffn_gain[:], post_ffn_norm.rearrange("(a n) -> a n", a=1).to_broadcast([P, D]))\
                .then_inc(ffn_gain_loaded, 16)
            pool.wait_ge(ffn_gain_loaded, 16)

        @block.scalar
        def _(act):
            own = Own(act, act_own)
            A = nc.scalar.activation

            def split(turn, half, width=W, wide_chunk=False):
                if turn.first == LAT_T and half == 0:
                    act.wait_ge(first_half_loaded, 16)
                else:
                    act.wait_ge(chunk_loaded[turn.slot()], turn.loaded())
                freed = turn.half_freed(half)
                if not isinstance(freed, int) or freed > 0:
                    act.wait_ge(halves_used, freed)
                A(hi[:, turn.half_slot(half), :, 0:width], raw_half(turn, half, width, wide_chunk),
                  ACT.Copy).then_inc(hi_ready, 1)

            act.wait_ge(consts, 1)
            A(col(RS_L), col(ONE_C), ACT.Sqrt)
            for t in range(TT):
                act.wait_ge(x_loaded[2 * t], 16)
                own.done(A(junk[:, 0:1024], xs[:, t, half_row(0)], ACT.Square, accum_out=col(SS_1 + 2 * t)))
                A(col(SS_X + t), col(SS_1 + 2 * t), ACT.Identity, scale=1.0 / D, bias=col(EPS_C))
                act.wait_ge(x_loaded[2 * t + 1], 16)
                own.done(A(junk[:, 1024:D], xs[:, t, half_row(1)], ACT.Square, accum_out=col(SS_1 + 2 * t + 1)))
                A(col(RS_X + t), col(SS_1 + 2 * t + 1), ACT.Sqrt, scale=1.0 / D,
                  bias=col(SS_X + t)).then_inc(roots, 1)

            def parts_high(dst, n, first_turn, gain0):
                act.wait_ge(turned, first_turn + (TT * 4 + 2 * n + 2 if n < 4 else 4 * (n + 1)))
                for v in range(2):
                    k = 2 * n + v
                    A(dst[:, k, 0, :], ps[:, 4 + n % 4, 256 * v:256 * v + 256], ACT.Copy,
                      scale=gcol[:, gain0 + k:gain0 + k + 1]).then_inc(parts_hi, 1)

            def evac_lat(j):
                act.wait_ge(halves_used, halves_by(LAT_T + 4 * j + 3))
                c0, width = (0, W) if j == 0 else (W, LAT_COLS - W)
                A(lat_nat[:, 0, c0:c0 + width], ps[:, 2 * j, 0:width], ACT.Copy).then_inc(mix_act, 1)

            def evac_t0(job, turn, dst, width):
                act.wait_ge(halves_used, halves_by(turn))
                A(dst, ps[:, 2 * (job % 2), 0:width], ACT.Copy).then_inc(mix_act, 1)

            def evac_kv(j):
                act.wait_ge(halves_used, halves_by(UKV_T + j // 2, j % 2 + 1))
                keys, values = kv_bank(2 * (j % 2))
                A(k_nat[:, 0, 2 * j:2 * j + 2, :], keys, ACT.Copy)
                A(v_mla[:, 0, 2 * j:2 * j + 2, :], values, ACT.Copy).then_inc(mix_act, 1)

            def fqk_evac(j):
                act.wait_ge(halves_used, halves_by(FQK_T + 4 * j + 3))
                A(fqk_to(j, 0), heads_in_bank(2 * (j % 2)), ACT.Copy).then_inc(mix_act, 1)

            split(Turn(LAT_T), 0)
            act.wait_ge(columns_ready, 1)
            for j, width in enumerate((W, LAT_COLS - W)):
                for n in range(8):
                    if j > 0 or n > 0:
                        split(Turn(LAT_T + 4 * j + n // 2), n % 2, width)
                    if j == 0:
                        parts_high(hT, n, 0, 0)
                    if j == 1 and n == 3:
                        evac_lat(0)
                    if j == 1 and n == 5:
                        act.wait_ge(angles_ready, 2)
                        A(cos_sin(0), angle[:, 1], ACT.Sin).then_inc(sines_ready, 1)
                        A(cos_sin(1), angle[:, 2], ACT.Sin).then_inc(sines_ready, 1)
            for j in range(FV_BLOCKS):
                for n in range(8):
                    split(Turn(FV_T + 4 * j + n // 2), n % 2, FV_W)
                    if n == 3 and j == 0:
                        evac_lat(1)
                    elif n == 3:
                        evac_t0(1 + j, FV_T + 4 * j - 1, vf[:, 0, FV_W * (j - 1):FV_W * j], FV_W)
                    if j == 0 and n == 5:
                        act.wait_ge(mix_act, 2)
                        act.wait_ge(mix_dve, 2)
                        for t in range(TT):
                            A(junk[:, 0:Q_LORA], lat_nat[:, t, 0:Q_LORA], ACT.Square, accum_out=col(SS_L + t))
                            own.done(A(junk[:, 512:768], lat_nat[:, t, Q_LORA:Q_LORA + KV_LORA], ACT.Square,
                                       accum_out=col(SS_L + 2 + t)))
                        A(col(RS_L, 2), col(SS_L, 2), ACT.Sqrt, scale=1.0 / Q_LORA, bias=col(EPS_C))
                        A(col(RS_L + 2, 2), col(SS_L + 2, 2), ACT.Sqrt, scale=1.0 / KV_LORA,
                          bias=col(EPS_C)).then_inc(roots, 1)
                    if j == 1 and n == 5:
                        for k in range(LAT_TILES):
                            act.wait_ge(turned, 2 * KT + 2 * (k - k % 2) + 4)
                            A(latT[:, k, 0, :], ps[:, 4 + k // 2, 256 * (k % 2):256 * (k % 2) + 256], ACT.Copy,
                              scale=gcol[:, 32 + k:33 + k]).then_inc(parts_hi, 1)
            for j in range(3):
                for n in range(2):
                    split(Turn(UQ_T + j), n)
                if j == 1:
                    evac_t0(4, FV_T + 11, vf[:, 0, FV_W * 2:FV_W * 3], FV_W)
                if j == 2:
                    evac_t0(5, UQ_T, q_flat(0, 0), W)
            for j in range(4):
                split(Turn(UKV_T + j // 2), j % 2, W, True)
                if j > 0:
                    evac_t0(5 + j, UQ_T + j, q_flat(0, j), W) if j < 3 else evac_kv(0)
            evac_kv(1)
            for j in range(4):
                for n in range(8):
                    split(Turn(FQK_T + 4 * j + n // 2), n % 2)
                    if j == 0 and n < 2:
                        evac_kv(2 + n)
                    if j == 1 and n == 2:
                        act.wait_ge(forget_abs, 1)
                        own.done(A(fgt[:, 2], fgt[:, 1], ACT.Exp, scale=-1.0))
                        A(fgt[:, 2], fgt[:, 2], ACT.Ln, bias=col(ONE_C)).then_inc(forget_soft, 1)
                    if j > 0 and n == 3:
                        fqk_evac(j - 1)
                    r = (8 * j + n - 5) // 2
                    if (8 * j + n - 5) % 2 == 0 and 0 <= r < 12 and r % 2 == 0:
                        act.wait_ge(items_turned, r + 1)
                        A(item_to(r), item_from(r), ACT.Copy).then_inc(items_act, 1)

            def gate_job(p, s, span, prev):
                h = p * 2 + s
                for n in range(8):
                    split(Turn(GATES_T + 4 * s + n // 2, 8, p, span), n % 2)
                    if n == 3:
                        if prev == "fqk":
                            fqk_evac(3)
                        else:
                            for t in range(TT):
                                act.wait_ge(gate_sum, h * 2 + (t - 1))
                                g = gates[:, t, cols(h * W - W)]
                                A(g, g, ACT.Tanh, scale=0.5).then_inc(gates_ready, 1)
                    if n == 4:
                        act.wait_ge(shifts_ready, h + 1)
                        if not isinstance(h, int) or h > 0:
                            act.wait_ge(probs_turned, h)
                        for b, sc in enumerate((SCALE_MLA, SCALE_FOX)):
                            for q in range(TT):
                                w = slice(128 * q, 128 + 256 * q)
                                last = A(probs[:, b, w], ps[:, 4 + b, w], ACT.Exp, scale=sc,
                                         bias=col(NB + 2 * b + q), accum_out=col(SUM + 2 * b + q))
                            last.then_inc(probs_raw, 1)
                    if n == 7:
                        act.wait_ge(probs_turned, h + 1)
                        A(probsT[:, 0, :], ps[:, 6, 0:384], ACT.Copy).then_inc(probsT_act, 1)
                act.wait_ge(heads_done, h + 1)
                A(o_mlaT[:, h, 0, :], ps[:, 4, 0:SEQ], ACT.Copy).then_inc(heads_hi, 1)
                A(o_foxT[:, h, 0, :], ps[:, 5, 0:SEQ], ACT.Copy).then_inc(heads_hi, 1)

            gate_job(0, 0, None, "fqk")
            gate_job(0, 1, None, "gate")
            with act.Fori(1, 4) as p:
                for s in range(2):
                    gate_job(p, s, range(1, 4), "gate")

            def merged_evac(c):
                for u in range(2):
                    act.wait_ge(merged_turned, 2 * c + u + 1)
                    A(mergedT[:, 4 * c + 2 * u:4 * c + 2 * u + 2, 0, :],
                      ps[:, 4 + (2 * c + u) % 4, :].rearrange("p (k q) -> p k q", k=2),
                      ACT.Copy, scale=0.5).then_inc(merged_hi, 1)

            for c in range(4):
                for n in range(8):
                    split(Turn(BRANCH_T + 4 * c + n // 2), n % 2)
                    if c == 0 and n == 3:
                        for t in range(TT):
                            act.wait_ge(gate_sum, 2 * 7 + t + 1)
                            g = gates[:, t, 7 * W:8 * W]
                            A(g, g, ACT.Tanh, scale=0.5).then_inc(gates_ready, 1)
                    if c > 0 and n == 6:
                        merged_evac(c - 1)

            def out_squares(j):
                act.wait_ge(halves_used, halves_by(OUT_T + 4 * j + 3))
                for t in (1, 0):
                    if t == 0:
                        act.wait_ge(out_evac, 2 * j + 1)
                    A(junk[:, W * t:W * t + W], ps[:, 2 * (j % 2) + t, :], ACT.Square,
                      accum_out=col(SS_O + 4 * t + j)).then_inc(out_sq, 1)

            for j in range(4):
                for n in range(8):
                    split(Turn(OUT_T + 4 * j + n // 2), n % 2)
                    if j == 0 and n == 5:
                        merged_evac(3)
                    if j > 0 and n == 3:
                        out_squares(j - 1)
                    if j == 3 and n == 5:
                        A(col(RS_L), col(ONE_C), ACT.Sqrt)
            def res_root(t):
                act.wait_ge(squares, t + 2 if t == 0 else 4)
                A(col(RS_1 + t), col(RS_1 + t), ACT.Sqrt, scale=1.0 / D, bias=col(EPS_C)).then_inc(roots, 1)

            for t in range(TT):
                if t == 0:
                    act.wait_ge(tile0_summed, 1)
                else:
                    act.wait_ge(halves_used, halves_by(OUT_T + 15))
                A(junk[:, W * t:W * t + W], ps[:, 2 + t, :], ACT.Square, accum_out=col(SS_O + 4 * t + 3))\
                    .then_inc(out_sq, 1)
                if t == 1:
                    res_root(0)
                act.wait_ge(squares, 2 * t + 1)
                A(col(RS_X + t), col(SS_X + t), ACT.Sqrt, scale=1.0 / D, bias=col(EPS_C)).then_inc(roots, 1)
                if t == 0:
                    split(Turn(UP_T), 0)
                else:
                    act.wait_ge(tile0_scale, 1)
                    A(y_mix[:, 0, half_row(0)], xs[:, 0, half_row(0)], ACT.Copy, scale=col(RS_1))\
                        .then_inc(tile0_normed, 1)
                for b in range(4):
                    act.wait_ge(res_ready, 4 * t + b + 1)
                    A(sum_junk[:, W * b:W * b + W], xs[:, t, W * b:W * b + W], ACT.Square,
                      accum_out=col(SS_1 + 4 * t + b)).then_inc(res_sq, 1)
            res_root(1)
            split(Turn(UP_T), 1)

            def low_parts(job, unit, turn, bank):
                act.wait_ge(halves_used, turn.upto(1))
                n = job * 2 + unit
                if not isinstance(n, int) or n > 0:
                    act.wait_ge(ffn_evac, n)
                b = bank + 2 * unit
                A(u_low[:], ps[:, b:b + 2, 256:512], ACT.Copy).then_inc(u_low_ready, 1)

            def gelu(i, unit):
                act.wait_ge(conv_ready, i * 4 + (unit + 1))
                A(gate_act[:, k_tiles(i, unit), 1, :], conv[:], ACT.Gelu_apprx_tanh).then_inc(act_took_conv, 1)

            def ff_hi(i, unit):
                act.wait_ge(conv_ready, i * 4 + (unit + 3))
                A(ffT[:, k_tiles(i, unit), 0, :], conv[:], ACT.Copy).then_inc(act_took_conv, 1)

            def up_job(i, s, span, prev):
                for n in range(8):
                    if isinstance(i, int) and s == 0:
                        if n >= 4:
                            split(Turn(UP_T + n // 2), n % 2)
                        parts_high(h2T, n, 2 * KT + 2 * LAT_TILES, KT)
                        if n < 2:
                            split(Turn(UP_T + 1), n)
                    else:
                        split(Turn(UP_T + 4 * s + n // 2, 8, i, span), n % 2)
                    if prev:
                        up_evac_act(i, s, span, n)

            def up_evac_act(i, s, span, n):
                if s == 1:
                    done, job, bank, step, who = Turn(UP_T + 3, 8, i, span), i * 2, 0, gelu, i
                else:
                    done, job, bank, step, who = Turn(UP_T - 1, 8, i, span), i * 2 - 1, 4, ff_hi, i - 1
                if n in (3, 5):
                    low_parts(job, (n - 3) // 2, done, bank)
                if n in (4, 6):
                    step(who, (n - 4) // 2)

            up_job(0, 0, None, False)
            up_job(0, 1, None, True)
            with act.Fori(1, QUADS) as i:
                for s in range(2):
                    up_job(i, s, range(1, QUADS), True)

            def down_squares(j):
                act.wait_ge(halves_used, halves_by(down_turn(j) + DOWN_CHUNKS - 1))
                for t in (1, 0):
                    if t == 0:
                        act.wait_ge(ffn_evac, 4 * QUADS + 2 * j + 1)
                    A(ffn_junk[:, W * t:W * t + W], ps[:, 2 * (j % 2) + t, :], ACT.Square,
                      accum_out=col(SS_O + 4 * t + j)).then_inc(down_sq, 1)

            for j in range(4):
                for n in range(2 * DOWN_CHUNKS):
                    split(Turn(down_turn(j) + n // 2), n % 2)
                    if j == 0:
                        up_evac_act(QUADS, 0, None, n)
                    elif n == 3:
                        down_squares(j - 1)
                    if j == 3 and n == 8:
                        A(col(RS_L), col(ONE_C), ACT.Sqrt)
            for t in range(TT):
                if t == 0:
                    act.wait_ge(tile0_summed, 3)
                else:
                    act.wait_ge(halves_used, halves_by(END_T - 1))
                A(ffn_junk[:, W * t:W * t + W], ps[:, 2 + t, :], ACT.Square, accum_out=col(SS_O + 4 * t + 3))\
                    .then_inc(down_sq, 1)
                act.wait_ge(squares, 2 * TT + t + 1)
                A(col(RS_X + t), col(SS_X + t), ACT.Sqrt, scale=1.0 / D, bias=col(EPS_C)).then_inc(roots, 1)

        @block.vector
        def _(dve):
            own = Own(dve, dve_own)
            V = nc.vector
            STT = nc.vector.scalar_tensor_tensor

            def split(turn, half, width=W, wide_chunk=False):
                dve.wait_ge(hi_ready, turn.upto(half))
                V.tensor_tensor(lo[:, turn.half_slot(half), :, 0:width],
                                raw_half(turn, half, width, wide_chunk),
                                hi[:, turn.half_slot(half), :, 0:width].bitcast(F32), ALU.subtract).then_inc(lo_ready, 1)

            def norm_x(t, b):
                xb = xs[:, t, half_row(b)]
                V.tensor_scalar(xb, xb, col(RS_X + t), None, ALU.mult).then_inc(normed, 1)

            for t in range(TT):
                dve.wait_ge(roots, t + 1)
                own.done(V.reciprocal(col(RS_X + t), col(RS_X + t)))
                for b in range(2 - t):
                    norm_x(t, b)
                if t == 0:
                    dve.wait_ge(columns_done, 1)
                    V.tensor_copy(gcol[:, 0:38], ps[:, 0, 0:38]).then_inc(columns_ready, 1)
            split(Turn(LAT_T), 0)

            def low_of(dst, bank, half, gain):
                STT(out=dst[:, 1, :], in0=ps[:, bank, 256 * half:256 * half + 256], scalar=gain,
                    in1=dst[:, 0, :].bitcast(F32), op0=ALU.mult, op1=ALU.subtract).then_inc(parts_lo, 1)

            def parts_low(dst, n, before, gain0):
                dve.wait_ge(parts_hi, before + 2 * n + 2)
                for v in range(2):
                    k = 2 * n + v
                    low_of(dst[:, k], 4 + n % 4, v, gcol[:, gain0 + k:gain0 + k + 1])

            def rope_angles():
                dve.wait_ge(rope_loaded, 32)
                own.done(V.tensor_copy(col(RS_X, 2), pos_i[:]))
                for t in range(TT):
                    own.done(V.tensor_scalar(angle[:, 0, t, :], inv_sb[:], col(RS_X + t), None, ALU.mult))
                parts = (6.28125, 507 / 2.0 ** 18, 2 * math.pi - 6.28125 - 507 / 2.0 ** 18)
                magic = 1.5 * 2.0 ** 23
                for j, quarter in ((1, 0.0), (2, 0.25)):
                    turns, r = angle[:, 3], angle[:, j]
                    own.done(V.tensor_scalar(turns, angle[:, 0], 1 / (2 * math.pi), quarter, ALU.mult, ALU.add))
                    own.done(V.tensor_scalar(turns, turns, magic, None, ALU.add))
                    own.done(V.tensor_scalar(turns, turns, magic, None, ALU.subtract))
                    own.done(STT(out=r, in0=turns, scalar=-parts[0], in1=angle[:, 0], op0=ALU.mult, op1=ALU.add))
                    own.done(STT(out=r, in0=turns, scalar=-parts[1], in1=r, op0=ALU.mult, op1=ALU.add))
                    own.done(STT(out=r, in0=turns, scalar=-parts[2], in1=r, op0=ALU.mult, op1=ALU.add))
                    if quarter:
                        own.done(V.tensor_scalar(r, r, math.pi / 2, None, ALU.add))
                    V.tensor_scalar(r, r, 3.1415925, -3.1415925, ALU.min, ALU.max).then_inc(angles_ready, 1)

            def evac_t1(job, turn, dst, width):
                dve.wait_ge(halves_used, halves_by(turn))
                V.tensor_copy(dst, ps[:, 2 * (job % 2) + 1, 0:width]).then_inc(mix_dve, 1)

            def rope(dst, src, cos, sin, tmp):
                (d1, d2), (s1, s2) = dst, src
                V.tensor_tensor(tmp[0], s1, cos, ALU.mult)
                V.tensor_tensor(tmp[1], s2, sin, ALU.mult)
                V.tensor_tensor(tmp[2], s2, cos, ALU.mult)
                own.done(V.tensor_tensor(tmp[3], s1, sin, ALU.mult))
                V.tensor_tensor(d1, tmp[0], tmp[1], ALU.subtract)
                return V.tensor_tensor(d2, tmp[2], tmp[3], ALU.add)

            for j, width in enumerate((W, LAT_COLS - W)):
                for n in range(8):
                    if j > 0 or n > 0:
                        split(Turn(LAT_T + 4 * j + n // 2), n % 2, width)
                    if j == 0:
                        parts_low(hT, n, 0, 0)
                        if n == 0:
                            norm_x(1, 1)
                    if j == 1 and n == 1:
                        rope_angles()
                    if j == 1 and n == 3:
                        evac_t1(0, LAT_T + 3, lat_nat[:, 1, 0:W], W)
                    if j == 1 and n == 6:
                        dve.wait_ge(columns_done, 2)
                        V.tensor_copy(convp[:].rearrange("p j f -> p (j f)"), ps[:, 4, 0:4 * 88])\
                         .then_inc(columns_ready, 1)
            H2 = ROPE // 2
            for j in range(FV_BLOCKS):
                for n in range(8):
                    split(Turn(FV_T + 4 * j + n // 2), n % 2, FV_W)
                    if n == 3 and j == 0:
                        evac_t1(1, LAT_T + 7, lat_nat[:, 1, W:LAT_COLS], LAT_COLS - W)
                    elif n == 3:
                        evac_t1(1 + j, FV_T + 4 * j - 1, vf[:, 1, FV_W * (j - 1):FV_W * j], FV_W)
                    if j == 0 and n == 6:
                        dve.wait_ge(roots, 3)
                        own.done(V.reciprocal(col(RS_L, 4), col(RS_L, 4)))
                        for t in range(TT):
                            q, kv = lat_nat[:, t, 0:Q_LORA], lat_nat[:, t, Q_LORA:Q_LORA + KV_LORA]
                            V.tensor_scalar(q, q, col(RS_L + t), None, ALU.mult)
                            V.tensor_scalar(kv, kv, col(RS_L + 2 + t), None, ALU.mult).then_inc(normed, 1)
                    if j == 0 and n == 7:
                        dve.wait_ge(sines_ready, 2)
                        for t in range(TT):
                            k1 = lat_nat[:, t, 768:768 + H2]
                            k2 = lat_nat[:, t, 768 + H2:768 + ROPE]
                            tmp = [rope_tmp[:, i, t, 0, :] for i in range(4)]
                            own.done(rope((kpe_nat[:, t, 0, 0:H2], kpe_nat[:, t, 0, H2:ROPE]), (k1, k2),
                                          cossin[:, 1, t, :], cossin[:, 0, t, :], tmp))
                            V.tensor_copy(kpe_nat[:, t, 1, :], kpe_nat[:, t, 0, :]).then_inc(kpe_roped, 1)
                    if j == 1 and n == 5:
                        for k in range(LAT_TILES):
                            dve.wait_ge(parts_hi, KT + k - k % 2 + 2)
                            low_of(latT[:, k], 4 + k // 2, k % 2, gcol[:, 32 + k:33 + k])
            for j in range(3):
                for n in range(2):
                    split(Turn(UQ_T + j), n)
                if j == 1:
                    evac_t1(4, FV_T + 11, vf[:, 1, FV_W * 2:FV_W * 3], FV_W)
                if j == 2:
                    evac_t1(5, UQ_T, q_flat(1, 0), W)

            def evac_kv(j):
                dve.wait_ge(halves_used, halves_by(UKV_T + j // 2, j % 2 + 1))
                keys, values = kv_bank(2 * (j % 2) + 1)
                V.tensor_copy(k_nat[:, 1, 2 * j:2 * j + 2, :], keys)
                V.tensor_copy(v_mla[:, 1, 2 * j:2 * j + 2, :], values).then_inc(mix_dve, 1)

            def fqk_evac(j):
                dve.wait_ge(halves_used, halves_by(FQK_T + 4 * j + 3))
                V.tensor_copy(fqk_to(j, 1), heads_in_bank(2 * (j % 2) + 1)).then_inc(mix_dve, 1)

            for j in range(4):
                split(Turn(UKV_T + j // 2), j % 2, W, True)
                if j > 0:
                    evac_t1(5 + j, UQ_T + j, q_flat(1, j), W) if j < 3 else evac_kv(0)
            evac_kv(1)

            def rope_queries(t):
                s1, s2 = q_nat[:, t, :, HD:HD + H2], q_nat[:, t, :, HD + H2:QH]
                cos = cossin[:, 1, t, :].unsqueeze(1).to_broadcast([P, HEADS, H2])
                sin = cossin[:, 0, t, :].unsqueeze(1).to_broadcast([P, HEADS, H2])
                tmp = [rope_tmp[:, i, t] for i in range(4)]
                rope((qpe_nat[:, t, :, 0:H2], qpe_nat[:, t, :, H2:ROPE]), (s1, s2), cos, sin, tmp)\
                    .then_inc(q_roped, 1)

            for j in range(4):
                for n in range(8):
                    split(Turn(FQK_T + 4 * j + n // 2), n % 2)
                    if j == 0 and n < 2:
                        evac_kv(2 + n)
                    if j == 1 and n == 1:
                        dve.wait_ge(mix_act, 5)
                        dve.wait_ge(mix_dve, 5)
                        dve.wait_ge(bfor_loaded, 16)
                        own.done(V.tensor_tensor(fgt[:, 0], vf[:, :, HEADS * HD:FV_COLS],
                                                 bfor[:].unsqueeze(1).to_broadcast([P, TT, HEADS]), ALU.add))
                        STT(out=fgt[:, 1], in0=fgt[:, 0], scalar=-1.0, in1=fgt[:, 0], op0=ALU.mult,
                            op1=ALU.max).then_inc(forget_abs, 1)
                    if j == 0 and n in (4, 6):
                        if n == 4:
                            dve.wait_ge(sines_ready, 2)
                            dve.wait_ge(mix_act, 8)
                            dve.wait_ge(mix_dve, 8)
                        rope_queries(n // 2 - 2)
                    if j == 1 and n == 4:
                        dve.wait_ge(forget_soft, 1)
                        V.memset(log_forget[:], 0.0)
                        own.done(STT(out=fgt[:, 3], in0=fgt[:, 0], scalar=0.0, in1=fgt[:, 2], op0=ALU.min,
                                     op1=ALU.subtract))
                        for r in range(0, DECAY_ROWS, 32):
                            ins = V.tensor_copy(log_forget[:, :, r:r + HEADS], fgt[:, 3])
                        ins.then_inc(forget_ready, 1)
                        own.done(V.tensor_tensor(head_of_row[:], ident[0:DECAY_ROWS, 0:HEADS],
                                                 ident[0:DECAY_ROWS, 32:32 + HEADS], ALU.add))
                        own.done(V.tensor_tensor(head_of_row[:], head_of_row[:],
                                                 ident[0:DECAY_ROWS, 64:64 + HEADS], ALU.add))
                    if j > 0 and n == 3:
                        fqk_evac(j - 1)
                    r = (8 * j + n - 5) // 2
                    if (8 * j + n - 5) % 2 == 0 and 0 <= r < 12 and r % 2 == 1:
                        dve.wait_ge(items_turned, r + 1)
                        if r < 11:
                            V.tensor_copy(item_to(r), item_from(r)).then_inc(items_dve, 1)
                        else:
                            own.done(V.tensor_scalar(negc[:], ps[0:DECAY_ROWS, 7, 0:SEQ], -1.0 / SCALE_FOX, None,
                                                     ALU.mult))
                            own.done(V.tensor_copy(decay_parts[:], negc[:]))
                            own.done(V.tensor_tensor(negc[:], negc[:], decay_parts[:], ALU.subtract))
                            V.tensor_copy(decay_parts[32:64], negc[32:64])
                            third, rest = decay_parts[64:DECAY_ROWS], negc[64:DECAY_ROWS]
                            own.done(V.tensor_copy(third, rest))
                            own.done(V.tensor_tensor(rest, rest, third, ALU.subtract))
                            V.tensor_copy(third, rest).then_inc(decay_ready, 1)
                            V.tensor_copy(small[:, CQ:CQ + 16].rearrange("p (h t) -> p t h", t=TT),
                                          ps[:, 7, SEQ:SEQ + 16].rearrange("p (t h) -> p t h", t=TT))\
                             .then_inc(decay_ready, 1)

            def gate_job(p, s, span, prev):
                h = p * 2 + s
                for n in range(8):
                    if n == 5:
                        dve.wait_ge(probs_raw, h * 2 + 2)
                        own.done(V.reciprocal(col(SUM, 4), col(SUM, 4)))
                        for b in range(2):
                            for q in range(TT):
                                w = probs[:, b, 128 * q:128 + 256 * q]
                                last = V.tensor_scalar(w, w, col(SUM + 2 * b + q), None, ALU.mult)
                        last.then_inc(probs_ready, 1)
                    split(Turn(GATES_T + 4 * s + n // 2, 8, p, span), n % 2)
                    if n == 3:
                        if prev == "fqk":
                            fqk_evac(3)
                        else:
                            gate_evac(h - 1, 1 - s, p - 1 if s == 0 else p,
                                      Turn(GATES_T + 4 * s - 1, 8, p, span).upto(1))
                    if n == 4:
                        dve.wait_ge(scores_done, h + 1)
                        for q in range(TT):
                            last = V.reduce_max(small[:, MX + q:MX + q + 3:2], ps[:, 4:6, 128 * q:128 + 256 * q], AX.X)
                        own.done(last)
                        cq = small[:, span_of(h * 2 + CQ, 2)]
                        V.tensor_scalar(col(NB, 2), col(MX, 2), -SCALE_MLA, None, ALU.mult)
                        own.done(STT(out=col(MX + 2, 2), in0=col(MX + 2, 2), scalar=SCALE_FOX, in1=cq,
                                     op0=ALU.mult, op1=ALU.add))
                        V.tensor_tensor(col(NB + 2, 2), cq, col(MX + 2, 2), ALU.subtract).then_inc(shifts_ready, 1)
                    if n == 7:
                        dve.wait_ge(probs_turned, h + 1)
                        V.tensor_copy(probsT[:, 1, :], ps[:, 7, 0:384]).then_inc(probsT_dve, 1)
                for b, o in enumerate((o_mlaT, o_foxT)):
                    dve.wait_ge(heads_hi, h * 2 + (b + 1))
                    V.tensor_tensor(o[:, one(h), 1, :].rearrange("p a q -> p (a q)"), ps[:, 4 + b, 0:SEQ],
                                    o[:, one(h), 0, :].rearrange("p a q -> p (a q)").bitcast(F32),
                                    ALU.subtract).then_inc(heads_lo, 1)

            def gate_evac(g, par, p, used):
                dve.wait_ge(halves_used, used)
                dve.wait_ge(bgate_loaded[par], p * 16 + 16)
                for t in range(TT):
                    V.tensor_tensor(gates[:, t, cols(g * W)], ps[:, 2 * par + t, :], bgate[:, par, :],
                                    ALU.add).then_inc(gate_sum, 1)

            gate_job(0, 0, None, "fqk")
            gate_job(0, 1, None, "gate")
            with dve.Fori(1, 4) as p:
                own.enter(p, 1, 6)
                for s in range(2):
                    gate_job(p, s, range(1, 4), "gate")
            own.leave(3)

            def branch_evac_job(c, b):
                dve.wait_ge(halves_used, halves_by(BRANCH_T + 4 * c + 2 * b + 1))
                dve.wait_ge(gates_ready, 2 * (4 * b + c) + 2)
                m = (m_mla, m_fox)[b]
                if b == 1 and c > 0:
                    dve.wait_ge(merged_turned, 2 * c)
                for t in range(TT):
                    ins = STT(out=m[:, t, :], in0=gates[:, t, D * b + W * c:D * b + W * c + W], scalar=1.0,
                              in1=ps[:, 2 * b + t, :], op0=ALU.add, op1=ALU.mult)
                    ins.then_inc(branch_evac, 1)
                if b == 1:
                    dve.wait_ge(branch_evac, 4 * c + 4)
                    V.tensor_tensor(m_fox[:], m_fox[:], m_mla[:], ALU.add).then_inc(merged_ready, 1)

            def merged_low(c):
                for u in range(2):
                    dve.wait_ge(merged_hi, 2 * c + u + 1)
                    k = 4 * c + 2 * u
                    STT(out=mergedT[:, k:k + 2, 1, :],
                        in0=ps[:, 4 + (2 * c + u) % 4, :].rearrange("p (k q) -> p k q", k=2), scalar=0.5,
                        in1=mergedT[:, k:k + 2, 0, :].bitcast(F32), op0=ALU.mult,
                        op1=ALU.subtract).then_inc(merged_lo, 1)

            for c in range(4):
                for n in range(8):
                    split(Turn(BRANCH_T + 4 * c + n // 2), n % 2)
                    if n == 3:
                        if c == 0:
                            gate_evac(7, 1, 3, halves_by(BRANCH_T - 1))
                        else:
                            branch_evac_job(c - 1, 1)
                    if n == 6 and c > 0:
                        merged_low(c - 1)
                    if n == 7:
                        branch_evac_job(c, 0)

            def out_evac_job(j):
                dve.wait_ge(halves_used, halves_by(OUT_T + 4 * j + 3))
                for t in range(TT):
                    if t == 1:
                        dve.wait_ge(out_sq, 2 * j + 1)
                    V.tensor_tensor(y_mix[:, t, W * j:W * j + W], ps[:, 2 * (j % 2) + t, :],
                                    mix_gain[:, W * j:W * j + W], ALU.mult).then_inc(out_evac, 1)

            for j in range(4):
                for n in range(8):
                    split(Turn(OUT_T + 4 * j + n // 2), n % 2)
                    if j == 0 and n == 3:
                        branch_evac_job(3, 1)
                    if j == 0 and n == 5:
                        merged_low(3)
                    if j > 0 and n == 3:
                        if j == 1:
                            dve.wait_ge(mix_gain_loaded, 16)
                        out_evac_job(j - 1)
            def total_square(t, sq, count):
                dve.wait_ge(sq, count)
                V.reduce_sum(col(SS_X + t), col(SS_O + 4 * t, 4), AX.X).then_inc(squares, 1)

            def norm_half(t, b):
                V.tensor_scalar(y_mix[:, t, half_row(b)], xs[:, t, half_row(b)], col(RS_1 + t), None,
                                ALU.mult).then_inc(normed, 1)

            for t in range(TT):
                total_square(t, out_sq, 6 + t + 1)
                V.tensor_tensor(y_mix[:, t, 3 * W:D], ps[:, 2 + t, :], mix_gain[:, 3 * W:D],
                                ALU.mult).then_inc(out_evac, 1)
                dve.wait_ge(out_evac, 6 + t + 1)
                dve.wait_ge(x_again, 16)
                dve.wait_ge(roots, (4, 6)[t])
                if t == 1:
                    V.reciprocal(col(RS_1), col(RS_1)).then_inc(tile0_scale, 1)
                own.done(V.reciprocal(col(RS_X + t), col(RS_X + t)))
                for b in range(4):
                    c = slice(W * b, W * b + W)
                    STT(out=xs[:, t, c], in0=y_mix[:, t, c], scalar=col(RS_X + t), in1=xs[:, t, c], op0=ALU.mult,
                        op1=ALU.add).then_inc(res_ready, 1)
                if t == 0:
                    split(Turn(UP_T), 0)
                dve.wait_ge(res_sq, 4 * t + 4)
                V.reduce_sum(col(RS_1 + t), col(SS_1 + 4 * t, 4), AX.X).then_inc(squares, 1)
            dve.wait_ge(roots, 7)
            own.done(V.reciprocal(col(RS_1 + 1), col(RS_1 + 1)))
            norm_half(1, 0)
            split(Turn(UP_T), 1)

            def tap(j, k):
                return convp[:, j, one(k)]

            def conv_unit(i, s, unit, banks, job):
                dve.wait_ge(u_low_ready, job * 2 + (unit + 1))
                b = banks + 2 * unit
                V.tensor_tensor(u_pad[:, :, 2:], ps[:, b:b + 2, 0:SEQ], u_low[:], ALU.add).then_inc(ffn_evac, 1)
                dve.wait_ge(ffn_evac, job * 2 + (unit + 1))
                took = job * 2 + unit
                if not isinstance(took, int) or took > 0:
                    dve.wait_ge(act_took_conv, took)
                k0 = i * 4 + (FF_TILES * s + 2 * unit)
                for v in range(2):
                    ins = V.tensor_scalar(conv[:, v, :], u_pad[:, v, 2:], tap(2, k0 + v), tap(3, k0 + v),
                                          ALU.mult, ALU.add)
                own.done(ins)
                for v in range(2):
                    ins = STT(out=conv[:, v, :], in0=u_pad[:, v, 1:SEQ + 1], scalar=tap(1, k0 + v),
                              in1=conv[:, v, :], op0=ALU.mult, op1=ALU.add)
                own.done(ins)
                for v in range(2):
                    ins = STT(out=conv[:, v, :], in0=u_pad[:, v, 0:SEQ], scalar=tap(0, k0 + v),
                              in1=conv[:, v, :], op0=ALU.mult, op1=ALU.add)
                if s == 0:
                    ins.then_inc(conv_ready, 1)
                else:
                    own.done(ins)
                    V.tensor_tensor(conv[:], conv[:], gate_act[:, k_tiles(i, unit), 1, :],
                                    ALU.mult).then_inc(conv_ready, 1)

            def ff_low(i, unit):
                dve.wait_ge(act_took_conv, i * 4 + (unit + 3))
                V.tensor_tensor(ffT[:, k_tiles(i, unit), 1, :], conv[:],
                                ffT[:, k_tiles(i, unit), 0, :].bitcast(F32), ALU.subtract).then_inc(ff_lo_ready, 1)

            def up_evac_dve(i, s, n):
                if n in (3, 5):
                    unit = (n - 3) // 2
                    if s == 1:
                        conv_unit(i, 0, unit, 0, i * 2)
                    else:
                        conv_unit(i - 1, 1, unit, 4, i * 2 - 1)
                if n in (4, 6) and s == 0:
                    ff_low(i - 1, (n - 4) // 2)

            def up_job(i, s, span, prev):
                for n in range(8):
                    if isinstance(i, int) and s == 0:
                        if n in (2, 3) or n >= 4:
                            split(Turn(UP_T + n // 2), n % 2)
                        parts_low(h2T, n, KT + LAT_TILES, KT)
                        if n == 0:
                            for t in range(TT):
                                norm_half(t, 1)
                    else:
                        split(Turn(UP_T + 4 * s + n // 2, 8, i, span), n % 2)
                    if prev:
                        up_evac_dve(i, s, n)

            up_job(0, 0, None, False)
            dve.wait_ge(consts, 6)
            up_job(0, 1, None, True)
            with dve.Fori(1, QUADS) as i:
                own.enter(i, 1, 10)
                for s in range(2):
                    up_job(i, s, range(1, QUADS), True)
            own.leave(QUADS - 1)

            def down_evac(j):
                dve.wait_ge(halves_used, halves_by(down_turn(j) + DOWN_CHUNKS - 1))
                for t in range(TT):
                    if t == 1:
                        dve.wait_ge(down_sq, 2 * j + 1)
                    V.tensor_tensor(y_ffn[:, t, W * j:W * j + W], ps[:, 2 * (j % 2) + t, :],
                                    ffn_gain[:, W * j:W * j + W], ALU.mult).then_inc(ffn_evac, 1)

            for j in range(4):
                for n in range(2 * DOWN_CHUNKS):
                    split(Turn(down_turn(j) + n // 2), n % 2)
                    if j == 0:
                        up_evac_dve(QUADS, 0, n)
                    elif n == 3:
                        if j == 1:
                            dve.wait_ge(ffn_gain_loaded, 16)
                        down_evac(j - 1)
            for t in range(TT):
                total_square(t, down_sq, 6 + t + 1)
                V.tensor_tensor(y_ffn[:, t, 3 * W:D], ps[:, 2 + t, :], ffn_gain[:, 3 * W:D],
                                ALU.mult).then_inc(ffn_evac, 1)
                dve.wait_ge(ffn_evac, 4 * QUADS + 6 + t + 1)
                dve.wait_ge(roots, 7 + t + 1)
                own.done(V.reciprocal(col(RS_X + t), col(RS_X + t)))
                for b in range(4):
                    c = slice(W * b, W * b + W)
                    STT(out=y_ffn[:, t, c], in0=y_ffn[:, t, c], scalar=col(RS_X + t), in1=xs[:, t, c],
                        op0=ALU.mult, op1=ALU.add).then_inc(y_ready, 1)

        @block.tensor
        def _(pe):
            mm = nc.tensor.matmul

            def rows_half(turn, half, aT, k0, bank, start, stop, width=W, n=2):
                pe.wait_ge(lo_ready, turn.upto(half))
                slot = turn.half_slot(half)
                for kk in range(n):
                    for t in range(TT):
                        acc = ps[:, bank + t, 0:width]
                        ah, al = (aT[:, k0 + kk, v, P * t:P * t + P] for v in range(2))
                        mm(acc, ah, hi[:, slot, kk, 0:width], start=start and kk == 0, stop=False)
                        mm(acc, ah, lo[:, slot, kk, 0:width], start=False, stop=False)
                        last = mm(acc, al, hi[:, slot, kk, 0:width], start=False, stop=stop and kk == n - 1)
                last.then_inc(halves_used, 1)

            def rows_last(turn, aT, k0, bank):
                for t in range(TT):
                    for n in range(4, 8):
                        own_turn = turn.plus(n // 2)
                        pe.wait_ge(lo_ready, own_turn.upto(n % 2))
                        slot = own_turn.half_slot(n % 2)
                        acc = ps[:, bank + t, :]
                        for kk in range(2):
                            ah, al = (aT[:, k0 + 2 * (n - 4) + kk, v, P * t:P * t + P] for v in range(2))
                            mm(acc, ah, hi[:, slot, kk, :], start=False, stop=False)
                            mm(acc, ah, lo[:, slot, kk, :], start=False, stop=False)
                            last = mm(acc, al, hi[:, slot, kk, :], start=False, stop=n == 7 and kk == 1)
                        if t == 1:
                            last.then_inc(halves_used, 1)
                    if t == 0:
                        last.then_inc(tile0_summed, 1)

            def turn_128(dst, src, rows=P):
                return nc.tensor.transpose(dst, src, ident[0:rows, 0:rows])

            def hold_clock(n, bank):
                for _ in range(n):
                    mm(ps[:, bank, P:2 * P], ident[:], ident[:], start=True, stop=True)

            pe.wait_ge(consts, 2)
            hold_clock(22, 3)
            pe.wait_ge(gains_loaded, 64)
            turn_128(ps[:, 0, 0:38], gain_rows[:], 38).then_inc(columns_done, 1)

            def turn_tile(src, t, k):
                c = 256 * (k % 2) + P * t
                turn_128(ps[:, 4 + k // 2 % 4, c:c + P], src[:, t, P * k:P * k + P]).then_inc(turned, 1)

            for t in range(TT):
                if t == 1:
                    hold_clock(3, 3)
                pe.wait_ge(normed, 2 * t + 1)
                for k in range(8):
                    turn_tile(xs, t, k)

            hold_clock(5, 3)

            def free_set(job):
                if job >= 2:
                    pe.wait_ge(mix_act, job - 1)
                    pe.wait_ge(mix_dve, job - 1)

            for j, width in enumerate((W, LAT_COLS - W)):
                for n in range(8):
                    if j == 0:
                        pe.wait_ge(parts_lo, 2 * n + 2)
                    if j == 0 and n == 0:
                        pe.wait_ge(columns_ready, 1)
                    rows_half(Turn(LAT_T + 4 * j + n // 2), n % 2, hT, 2 * n, 2 * j, n == 0, n == 7, width)
                    if j == 0 and n < 4:
                        pe.wait_ge(normed, 2 * TT)
                        for k in (8 + 2 * n, 9 + 2 * n):
                            for t in range(TT):
                                turn_tile(xs, t, k)
                    if j == 1 and n == 2:
                        pe.wait_ge(convs_loaded, 32)
                        for i in range(4):
                            last = turn_128(ps[:, 4, 88 * i:88 * i + 88], conv_rows[:, i, :], 88)
                        last.then_inc(columns_done, 1)
            for j in range(FV_BLOCKS):
                free_set(2 + j)
                for n in range(8):
                    rows_half(Turn(FV_T + 4 * j + n // 2), n % 2, hT, 2 * n, 2 * (j % 2), n == 0, n == 7, FV_W)
                    if j == 1 and n == 2:
                        pe.wait_ge(normed, 3 * TT)
                        pe.wait_ge(columns_ready, 2)
                        for k in range(LAT_TILES):
                            for t in range(TT):
                                c = 256 * (k % 2) + P * t
                                turn_128(ps[:, 4 + k // 2, c:c + P], lat_nat[:, t, P * k:P * k + P]).then_inc(turned, 1)
            pe.wait_ge(parts_lo, KT + LAT_TILES)
            for j in range(3):
                free_set(5 + j)
                for n in range(2):
                    rows_half(Turn(UQ_T + j), n, latT, 2 * n, 2 * ((5 + j) % 2), n == 0, n == 1)
            for j in range(4):
                free_set(8 + j)
                rows_half(Turn(UKV_T + j // 2), j % 2, latT, Q_LORA // P, 2 * (j % 2), True, True)

            def turn_item(r):
                if r >= 4:
                    pe.wait_ge(items_dve if r % 2 else items_act, (r - 4) // 2 + 1)
                bank = ps[:, 4 + r % 4, :]
                if r == 0:
                    pe.wait_ge(mix_act, 12)
                    pe.wait_ge(mix_dve, 12)
                if r == 4:
                    pe.wait_ge(kpe_roped, 2)
                if r == 5:
                    pe.wait_ge(q_roped, 2)
                if r == 11:
                    pe.wait_ge(forget_ready, 1)
                    pe.wait_ge(consts, 5)
                    f = [fgt[:, 3, t, :] for t in range(TT)]
                    tri, ones = tri_ones[:, 0:P], tri_ones[:, P:2 * P]
                    mm(bank[0:DECAY_ROWS, 0:SEQ], log_forget[:, 0, :], tri_ones[:], start=True, stop=False)
                    mm(bank[0:DECAY_ROWS, P:SEQ], log_forget[:, 1, :], tri, start=False, stop=True)
                    mm(bank[:, SEQ:SEQ + HEADS], tri, f[0], start=True, stop=True)
                    mm(bank[:, SEQ + HEADS:SEQ + 2 * HEADS], ones, f[0], start=True, stop=False)
                    mm(bank[:, SEQ + HEADS:SEQ + 2 * HEADS], tri, f[1], start=False, stop=True)\
                        .then_inc(items_turned, 1)
                    return
                for v in range(1 if r == 4 else 2):
                    for t in range(TT):
                        c = 256 * v + P * t
                        if r < 4:
                            src = k_nat[:, t, 2 * r + v, :]
                        elif r == 4:
                            src = kpe_nat[:, t].rearrange("p a d -> p (a d)")
                        elif r < 9:
                            src = q_nat[:, t, 2 * (r - 5) + v, 0:HD]
                        else:
                            h = 4 * (r - 9) + 2 * v
                            src = qpe_nat[:, t, h:h + 2, :].rearrange("p a d -> p (a d)")
                        last = turn_128(bank[:, c:c + P], src)
                last.then_inc(items_turned, 1)

            for j in range(4):
                free_set(12 + j)
                for n in range(8):
                    turn = Turn(FQK_T + 4 * j + n // 2)
                    pe.wait_ge(lo_ready, turn.upto(n % 2))
                    slot = turn.half_slot(n % 2)
                    for kk in range(2):
                        for f in range(4):
                            acc = ps[:, 2 * (j % 2) + f // 2, 256 * (f % 2):256 * (f % 2) + 256]
                            k = 2 * n + kk
                            first, final = n == 0 and kk == 0 and f % 2 == 0, n == 7 and kk == 1
                            wc = slice(P * f, P * f + P)
                            mm(acc, hi[:, slot, kk, wc], hT[:, k, 0, :], start=first, stop=False, skip_group_check=True)
                            mm(acc, hi[:, slot, kk, wc], hT[:, k, 1, :], start=False, stop=False, skip_group_check=True)
                            last = mm(acc, lo[:, slot, kk, wc], hT[:, k, 0, :], start=False, stop=final,
                                      skip_group_check=True)
                    last.then_inc(halves_used, 1)
                    if (8 * j + n) % 2 == 0 and (8 * j + n) // 2 < 12:
                        turn_item((8 * j + n) // 2)

            def scores(h, par):
                pe.wait_ge(q_staged, h + 1)
                if not isinstance(h, int) or h > 0:
                    pe.wait_ge(heads_hi, h * 2)
                    pe.wait_ge(heads_lo, h * 2)
                half = slice(64 * par, 64 * par + 64)
                for q in range(TT):
                    keys = P * (q + 1)
                    c, qs = P * q, slice(P * q, P * q + P)
                    acc = ps[:, 4, c:c + keys]
                    mm(acc, q_now[:, 0, qs], head(qkT, h, 1, keys), start=True, stop=False)
                    mm(acc, qpe_now[half, qs], kpeT[half, 0:keys], start=False, stop=False)
                    mm(ps[:, 4, c + keys - P:c + keys], ident_bf[:], mask_mla[:], start=False, stop=True)
                for q in range(TT):
                    keys = P * (q + 1)
                    c, qs = P * q, slice(P * q, P * q + P)
                    acc = ps[:, 5, c:c + keys]
                    mm(acc, q_now[:, 1, qs], head(fqkT, h, 1, keys), start=True, stop=False)
                    mm(acc, head_rows[:], decay_parts[:, 0:keys], start=False, stop=False)
                    last = mm(ps[:, 5, c + keys - P:c + keys], ident_bf[:], mask_fox[:], start=False, stop=True)
                last.then_inc(scores_done, 1)

            def head(t, h, which, n):
                return t[:, one(h), which, 0:n].rearrange("p a q -> p (a q)")

            def turn_probs(h):
                pe.wait_ge(probs_ready, h + 1)
                if not isinstance(h, int) or h > 0:
                    pe.wait_ge(probsT_act, h)
                    pe.wait_ge(probsT_dve, h)
                for b in range(2):
                    for c in range(3):
                        last = turn_128(ps[:, 6 + b, P * c:P * c + P], probs[:, b, P * c:P * c + P])
                last.then_inc(probs_turned, 1)

            def outputs(h):
                pe.wait_ge(v_staged, h + 1)
                pe.wait_ge(probsT_act, h + 1)
                pe.wait_ge(probsT_dve, h + 1)
                for b in range(2):
                    mm(ps[:, 4 + b, 0:SEQ], v_now[:, b, 0, :], probsT[:, b, 0:SEQ], start=True, stop=False)
                    last = mm(ps[:, 4 + b, P:SEQ], v_now[:, b, 1, :], probsT[:, b, SEQ:SEQ + P], start=False, stop=True)
                last.then_inc(heads_done, 1)

            def gate_job(p, s, span):
                h = p * 2 + s
                if isinstance(p, int):
                    free_set(16 + s)
                else:
                    pe.wait_ge(gate_sum, h * 2 - 2)
                scores(h, s)
                for n in range(8):
                    rows_half(Turn(GATES_T + 4 * s + n // 2, 8, p, span), n % 2, hT, 2 * n, 2 * s, n == 0, n == 7)
                    if n == 3:
                        turn_probs(h)
                    if n == 5:
                        outputs(h)

            gate_job(0, 0, None)
            gate_job(0, 1, None)
            with pe.Fori(1, 4) as p:
                for s in range(2):
                    gate_job(p, s, range(1, 4))

            def turn_merged(c):
                pe.wait_ge(merged_ready, c + 1)
                for u in range(2):
                    if 2 * c + u >= 4:
                        pe.wait_ge(merged_lo, 2 * c + u - 3)
                    for v in range(2):
                        for t in range(TT):
                            f = P * (2 * u + v)
                            last = turn_128(ps[:, 4 + (2 * c + u) % 4, 256 * v + P * t:256 * v + P * t + P],
                                            m_fox[:, t, f:f + P])
                    last.then_inc(merged_turned, 1)

            for c in range(4):
                for b, oT in enumerate((o_mlaT, o_foxT)):
                    if c == 0:
                        pe.wait_ge(gate_sum, 14 + 2 * b)
                        if b == 0:
                            pe.wait_ge(heads_lo, 2 * HEADS)
                            pe.wait_ge(heads_hi, 2 * HEADS)
                    else:
                        pe.wait_ge(branch_evac, 2 * (2 * c + b - 1))
                    for n in range(4):
                        rows_half(Turn(BRANCH_T + 4 * c + 2 * b + n // 2), n % 2, oT, 2 * n, 2 * b, n == 0, n == 3)
                        if b == 0 and n == 2 and c > 0:
                            turn_merged(c - 1)
            for j in range(4):
                if j < 2:
                    pe.wait_ge(branch_evac, 14 + 2 * j)
                else:
                    pe.wait_ge(out_evac, 2 * (j - 1))
                    pe.wait_ge(out_sq, 2 * (j - 1))
                for n in range(8 if j < 3 else 4):
                    if j == 0 and n % 2 == 0:
                        pe.wait_ge(merged_lo, n + 2)
                    rows_half(Turn(OUT_T + 4 * j + n // 2), n % 2, mergedT, 2 * n, 2 * (j % 2), n == 0, n == 7)
                    if j == 0 and n == 2:
                        turn_merged(3)
            rows_last(Turn(OUT_T + 12), mergedT, 8, 2)
            for t in range(TT):
                hold_clock(12, 7)
                if t == 0:
                    pe.wait_ge(tile0_normed, 1)
                else:
                    pe.wait_ge(normed, 3 * TT + 1)
                for k in range(8):
                    turn_tile(y_mix, t, k)
            pe.wait_ge(out_evac, 8)
            pe.wait_ge(out_sq, 8)
            hold_clock(5, 3)

            def up_half(turn, n, bank):
                pe.wait_ge(lo_ready, turn.upto(n % 2))
                slot = turn.half_slot(n % 2)
                for kk in range(2):
                    k = 2 * n + kk
                    for f in range(4):
                        wc = slice(P * f, P * f + P)
                        mm(ps[:, bank + f, :], hi[:, slot, kk, wc], h2T[:, k, :, :].rearrange("p a q -> p (a q)"),
                           start=k == 0, stop=False)
                        last = mm(ps[:, bank + f, 0:SEQ], lo[:, slot, kk, wc], h2T[:, k, 0, :],
                                  start=False, stop=k == KT - 1)
                last.then_inc(halves_used, 1)

            def up_job(i, s, span):
                if not isinstance(i, int):
                    pe.wait_ge(ffn_evac, i * 4 + (2 * s - 2))
                for n in range(8):
                    if isinstance(i, int) and s == 0:
                        pe.wait_ge(parts_lo, KT + LAT_TILES + 2 * n + 2)
                    up_half(Turn(UP_T + 4 * s + n // 2, 8, i, span), n, 4 * s)
                    if isinstance(i, int) and s == 0 and n < 4:
                        pe.wait_ge(normed, 3 * TT + 3)
                        for k in (8 + 2 * n, 9 + 2 * n):
                            for t in range(TT):
                                turn_tile(y_mix, t, k)

            up_job(0, 0, None)
            up_job(0, 1, None)
            with pe.Fori(1, QUADS) as i:
                for s in range(2):
                    up_job(i, s, range(1, QUADS))
            with pe.Fori(0, 2) as p:
                for s in range(2):
                    pe.wait_ge(ffn_evac, p * 4 + (4 * QUADS - 2 + 2 * s))
                    if s == 0:
                        pe.wait_ge(ff_lo_ready, 2 * (QUADS - 1))
                    for n in range(2 * DOWN_CHUNKS - 4 * s):
                        if n == 2 * DOWN_CHUNKS - 2:
                            pe.wait_ge(ff_lo_ready, 2 * QUADS)
                        rows_half(Turn(down_turn(s) + n // 2, 24, p, range(2)), n % 2, ffT, 2 * n, 2 * s,
                                  n == 0, n == 2 * DOWN_CHUNKS - 1)
                    if s == 1:
                        rows_last(Turn(down_turn(1) + DOWN_CHUNKS - 4, 24, p, range(2)), ffT, FF_TILES - 8, 2)


_INS = ["x", "positions", "pre_mix_norm", "w_in", "q_a_norm", "w_uq", "kv_a_norm", "w_ukv", "b_forget", "b_gate",
        "w_branch_mla", "w_branch_fox", "w_out", "post_mix_norm", "pre_ffn_norm", "w_up", "conv_w", "conv_b",
        "w_down", "post_ffn_norm"]


def kernel(**inputs):
    import numpy as _np
    import concourse.bacc as _bacc
    from concourse import mybir as _mybir
    from concourse.bass_utils import run_bass_kernel_spmd as _run

    nc = _bacc.Bacc("TRN2", target_bir_lowering=False, num_devices=1)
    arrays, args = {}, []
    freq = (1.0 / 10000.0 ** (_np.arange(0, ROPE, 2, dtype=_np.float32) / ROPE)).astype(_np.float32)[None, :]
    for name, a in [(n, _np.ascontiguousarray(inputs[n])) for n in _INS] + [("rope_freq", freq)]:
        arrays[f"in_{name}_dram"] = a
        args.append(nc.dram_tensor(f"in_{name}_dram", a.shape, _mybir.dt.from_np(a.dtype), kind="ExternalInput").ap())
    args.append(nc.dram_tensor("out_dram", (1, SEQ, D), F32, kind="ExternalOutput").ap())
    residual_block(nc, *args)
    r = _run(nc, [arrays], core_ids=[0])
    return r.results[0]["out_dram"]
```
